# Optimizing a Trainium2 kernel written in Bass

```python
import math
import jax
import jax.numpy as jnp
from jax import lax
import numpy as np
import jax, jax.numpy as jnp

D_MODEL = 1024
BATCH = 1
SEQ = 1024
DEPTH = 1

GLA_HEADS = 4
GLA_DK = D_MODEL // 16
GLA_DV = D_MODEL // 8
GLA_RANK = 16
GLA_GATE_NORM = 16.0
ML_HEADS = 4
ML_DK = D_MODEL // 16
ML_DV = D_MODEL // 8
ML_CONV = 4
S5_GROUP = 16
S5_WIDTH = D_MODEL // 2
S5_GROUPS = S5_WIDTH // S5_GROUP
S5_STATE = 64
S5_DT_MIN = 0.001
S5_DT_MAX = 0.1
CHUNK = 64
FFN_HIDDEN = ((8 * D_MODEL + 767) // 768) * 256
N_BRANCH = 3
RMS_EPS = 1e-6

IN_SIZES = (
    GLA_HEADS * GLA_DK,
    GLA_HEADS * GLA_DK,
    GLA_HEADS * GLA_DV,
    GLA_RANK,
    GLA_HEADS * GLA_DV,
    ML_HEADS * ML_DK,
    ML_HEADS * ML_DK,
    ML_HEADS * ML_DV,
    ML_HEADS,
    ML_HEADS,
    ML_HEADS * ML_DV,
    S5_WIDTH,
    N_BRANCH * D_MODEL,
)
IN_DIM = sum(IN_SIZES)


def rms_norm(x, w):
    xf = x.astype(jnp.float32)
    y = xf * lax.rsqrt(jnp.mean(xf * xf, axis=-1, keepdims=True) + RMS_EPS)
    return (y * w.astype(jnp.float32)).astype(x.dtype)

def _split(z, sizes):
    out, start = [], 0
    for s in sizes:
        out.append(z[..., start:start + s])
        start += s
    return out

def _heads(a, n):
    return a.reshape(a.shape[0], a.shape[1], n, -1)

def _to_chunks(a):
    b, t, h, d = a.shape
    return a.reshape(b, t // CHUNK, CHUNK, h, d).transpose(1, 0, 3, 2, 4)

def _from_chunks(a):
    n, b, h, l, d = a.shape
    return a.transpose(1, 0, 3, 2, 4).reshape(b, n * l, h, d)

def gla_attention(q, k, v, g):
    out_dtype = v.dtype
    f32 = jnp.float32
    bsz, _, heads, dk = q.shape
    dv = v.shape[-1]
    qc, kc, vc, gc = (_to_chunks(a.astype(f32)) for a in (q * dk ** -0.5, k, v, g))
    causal = jnp.tril(jnp.ones((CHUNK, CHUNK), dtype=bool))

    def step(state, inp):
        qi, ki, vi, gi = inp
        cum = jnp.cumsum(gi, axis=2)
        o_inter = jnp.einsum('bhld,bhdv->bhlv', qi * jnp.exp(cum), state)
        rel = cum[:, :, :, None, :] - cum[:, :, None, :, :]
        decay = jnp.exp(jnp.where(causal[:, :, None], rel, -jnp.inf))
        scores = jnp.einsum('bhid,bhjd,bhijd->bhij', qi, ki, decay)
        o = o_inter + jnp.einsum('bhij,bhjv->bhiv', scores, vi)
        last = cum[:, :, -1:, :]
        state = (jnp.exp(last[:, :, 0, :])[..., None] * state
                 + jnp.einsum('bhjd,bhjv->bhdv', ki * jnp.exp(last - cum), vi))
        return state, o

    s0 = jnp.zeros((bsz, heads, dk, dv), f32)
    _, o = lax.scan(step, s0, (qc, kc, vc, gc))
    return _from_chunks(o).astype(out_dtype)

def mlstm_memory(q, k, v, i_pre, f_pre):
    out_dtype = v.dtype
    f32 = jnp.float32
    bsz, _, heads, dk = q.shape
    dv = v.shape[-1]
    log_f = jax.nn.log_sigmoid(f_pre.astype(f32))
    qc, kc, vc = (_to_chunks(a.astype(f32)) for a in (q, k * dk ** -0.5, v))
    ic, fc = (_to_chunks(a.astype(f32)[..., None])[..., 0] for a in (i_pre, log_f))
    causal = jnp.tril(jnp.ones((CHUNK, CHUNK), dtype=bool))

    def step(carry, inp):
        mem, norm, m_prev = carry
        qi, ki, vi, ii, lfi = inp
        b = jnp.cumsum(lfi, axis=-1)
        a_inter = b + m_prev[..., None]
        d_intra = jnp.where(causal, b[..., :, None] - b[..., None, :] + ii[..., None, :], -jnp.inf)
        m_t = jnp.maximum(a_inter, jnp.max(d_intra, axis=-1))
        w_inter = jnp.exp(a_inter - m_t)
        scores = jnp.einsum('bhtd,bhsd->bhts', qi, ki) * jnp.exp(d_intra - m_t[..., None])
        num = (w_inter[..., None] * jnp.einsum('bhtd,bhdv->bhtv', qi, mem)
               + jnp.einsum('bhts,bhsv->bhtv', scores, vi))
        den = w_inter * jnp.einsum('bhtd,bhd->bht', qi, norm) + jnp.sum(scores, axis=-1)
        h = num / jnp.maximum(jnp.abs(den), jnp.exp(-m_t))[..., None]
        m_new = m_t[..., -1]
        carry_decay = jnp.exp(b[..., -1] + m_prev - m_new)
        w_key = jnp.exp(b[..., -1:] - b + ii - m_new[..., None])
        mem = carry_decay[..., None, None] * mem + jnp.einsum('bhs,bhsd,bhsv->bhdv', w_key, ki, vi)
        norm = carry_decay[..., None] * norm + jnp.einsum('bhs,bhsd->bhd', w_key, ki)
        return (mem, norm, m_new), h

    carry0 = (jnp.zeros((bsz, heads, dk, dv), f32),
              jnp.zeros((bsz, heads, dk), f32),
              jnp.zeros((bsz, heads), f32))
    _, h = lax.scan(step, carry0, (qc, kc, vc, ic, fc))
    return _from_chunks(h).astype(out_dtype)

def _complex_linear_combine(earlier, later):
    a1r, a1i, b1r, b1i = earlier
    a2r, a2i, b2r, b2i = later
    return (a2r * a1r - a2i * a1i,
            a2r * a1i + a2i * a1r,
            a2r * b1r - a2i * b1i + b2r,
            a2r * b1i + a2i * b1r + b2i)

def s5_ssm(u, lam_re, lam_im, log_step, b_re, b_im, c_re, c_im, d_skip):
    out_dtype = u.dtype
    f32 = jnp.float32
    bsz, t, _ = u.shape
    uf = u.astype(f32).reshape(bsz, t, S5_GROUPS, S5_GROUP)
    lam_re = jnp.minimum(lam_re.astype(f32), -1e-4)
    lam_im = lam_im.astype(f32)
    dt = jnp.exp(log_step.astype(f32))[:, None]
    mag = jnp.exp(lam_re * dt)
    abar_re = mag * jnp.cos(lam_im * dt)
    abar_im = mag * jnp.sin(lam_im * dt)
    inv = 1.0 / (lam_re * lam_re + lam_im * lam_im)
    z_re = ((abar_re - 1.0) * lam_re + abar_im * lam_im) * inv
    z_im = (abar_im * lam_re - (abar_re - 1.0) * lam_im) * inv
    b_re = b_re.astype(f32)
    b_im = b_im.astype(f32)
    bbar_re = z_re[..., None] * b_re - z_im[..., None] * b_im
    bbar_im = z_re[..., None] * b_im + z_im[..., None] * b_re
    bu_re = jnp.einsum('gpc,btgc->btgp', bbar_re, uf)
    bu_im = jnp.einsum('gpc,btgc->btgp', bbar_im, uf)
    a_re = jnp.broadcast_to(abar_re, (1, t) + abar_re.shape)
    a_im = jnp.broadcast_to(abar_im, (1, t) + abar_im.shape)
    _, _, x_re, x_im = lax.associative_scan(_complex_linear_combine, (a_re, a_im, bu_re, bu_im), axis=1)
    y = (jnp.einsum('gcp,btgp->btgc', c_re.astype(f32), x_re)
         - jnp.einsum('gcp,btgp->btgc', c_im.astype(f32), x_im))
    y = y.reshape(bsz, t, S5_WIDTH) + d_skip.astype(f32) * u.astype(f32)
    return y.astype(out_dtype)

def causal_dwconv(u, w, b):
    k = w.shape[0]
    y = lax.conv_general_dilated(u, w[:, None, :], window_strides=(1,), padding=[(k - 1, 0)],
                                 dimension_numbers=('NWC', 'WIO', 'NWC'),
                                 feature_group_count=u.shape[-1])
    return y + b

def hybrid_mixer(h, w_in, gla_a2, gla_a_b, gla_norm_w, ml_conv_w, ml_conv_b, ml_i_b, ml_f_b,
                 s5_lam_re, s5_lam_im, s5_log_step, s5_b_re, s5_b_im, s5_c_re, s5_c_im, s5_d,
                 s5_glu_w, s5_glu_b, proj_gla, proj_ml, proj_s5, branch_gate_b, w_out):
    bsz, t, _ = h.shape
    z = h @ w_in
    gq, gk, gv, ga, gr, mq, mk, mv, mi, mf, mo, su, zg = _split(z, IN_SIZES)

    g_log = jax.nn.log_sigmoid((ga @ gla_a2 + gla_a_b).astype(jnp.float32)) / GLA_GATE_NORM
    o_gla = gla_attention(_heads(gq, GLA_HEADS), _heads(gk, GLA_HEADS), _heads(gv, GLA_HEADS),
                          _heads(g_log, GLA_HEADS))
    o_gla = rms_norm(o_gla, gla_norm_w.reshape(GLA_HEADS, GLA_DV)).reshape(bsz, t, -1)
    y_gla = o_gla * jax.nn.silu(gr)

    qk = jax.nn.silu(causal_dwconv(jnp.concatenate([mq, mk], axis=-1), ml_conv_w, ml_conv_b))
    mq = qk[..., :ML_HEADS * ML_DK]
    mk = qk[..., ML_HEADS * ML_DK:]
    h_ml = mlstm_memory(_heads(mq, ML_HEADS), _heads(mk, ML_HEADS), _heads(mv, ML_HEADS),
                        mi + ml_i_b, mf + ml_f_b)
    y_ml = jax.nn.sigmoid(mo) * h_ml.reshape(bsz, t, -1)

    y_s5 = jax.nn.gelu(s5_ssm(su, s5_lam_re, s5_lam_im, s5_log_step, s5_b_re, s5_b_im,
                              s5_c_re, s5_c_im, s5_d))
    y_s5 = y_s5 * jax.nn.sigmoid(y_s5 @ s5_glu_w + s5_glu_b)

    gates = jax.nn.sigmoid(zg + branch_gate_b).reshape(bsz, t, N_BRANCH, D_MODEL)
    merged = (gates[:, :, 0] * (y_gla @ proj_gla)
              + gates[:, :, 1] * (y_ml @ proj_ml)
              + gates[:, :, 2] * (y_s5 @ proj_s5))
    return merged @ w_out

def swiglu_ffn(h, w_in, w_out):
    gate, up = jnp.split(h @ w_in, 2, axis=-1)
    return (jax.nn.silu(gate) * up) @ w_out

def first_inputs(seed: int = 0) -> dict:
    key = jax.random.key(seed)
    keys = list(jax.random.split(key, 48))

    def normal(shape, scale):
        return scale * jax.random.normal(keys.pop(), shape, jnp.float32)

    def uniform(shape):
        return jax.random.uniform(keys.pop(), shape, jnp.float32)

    def gain(shape):
        return 1.0 + normal(shape, 0.05)

    L, D = DEPTH, D_MODEL
    glw = GLA_HEADS * GLA_DV
    mlw = ML_HEADS * ML_DV
    n_idx = jnp.arange(S5_STATE, dtype=jnp.float32)
    log_lo, log_hi = math.log(S5_DT_MIN), math.log(S5_DT_MAX)
    return {
        'x': normal((BATCH, SEQ, D), 1.0),
        'c': normal((BATCH, D), 1.0),
        'ada_w': normal((L, D, 6 * D), 0.1 * D ** -0.5),
        'ada_b': normal((L, 6 * D), 0.01),
        'pre1_w': gain((L, D)),
        'post1_w': gain((L, D)),
        'pre2_w': gain((L, D)),
        'post2_w': gain((L, D)),
        'w_in': normal((L, D, IN_DIM), D ** -0.5),
        'gla_a2': normal((L, GLA_RANK, GLA_HEADS * GLA_DK), GLA_RANK ** -0.5),
        'gla_a_b': normal((L, GLA_HEADS * GLA_DK), 0.1),
        'gla_norm_w': gain((L, glw)),
        'ml_conv_w': normal((L, ML_CONV, 2 * ML_HEADS * ML_DK), ML_CONV ** -0.5),
        'ml_conv_b': normal((L, 2 * ML_HEADS * ML_DK), 0.01),
        'ml_i_b': normal((L, ML_HEADS), 0.1),
        'ml_f_b': 3.0 + 3.0 * uniform((L, ML_HEADS)),
        's5_lam_re': -0.5 + normal((L, S5_GROUPS, S5_STATE), 0.01),
        's5_lam_im': math.pi * n_idx + normal((L, S5_GROUPS, S5_STATE), 0.01),
        's5_log_step': log_lo + (log_hi - log_lo) * uniform((L, S5_GROUPS)),
        's5_b_re': normal((L, S5_GROUPS, S5_STATE, S5_GROUP), (2 * S5_GROUP) ** -0.5),
        's5_b_im': normal((L, S5_GROUPS, S5_STATE, S5_GROUP), (2 * S5_GROUP) ** -0.5),
        's5_c_re': normal((L, S5_GROUPS, S5_GROUP, S5_STATE), S5_STATE ** -0.5),
        's5_c_im': normal((L, S5_GROUPS, S5_GROUP, S5_STATE), S5_STATE ** -0.5),
        's5_d': normal((L, S5_WIDTH), 1.0),
        's5_glu_w': normal((L, S5_WIDTH, S5_WIDTH), S5_WIDTH ** -0.5),
        's5_glu_b': normal((L, S5_WIDTH), 0.01),
        'proj_gla': normal((L, glw, D), glw ** -0.5),
        'proj_ml': normal((L, mlw, D), mlw ** -0.5),
        'proj_s5': normal((L, S5_WIDTH, D), S5_WIDTH ** -0.5),
        'branch_gate_b': normal((L, N_BRANCH * D), 0.01),
        'w_out': normal((L, D, D), D ** -0.5),
        'ffn_w_in': normal((L, D, 2 * FFN_HIDDEN), D ** -0.5),
        'ffn_w_out': normal((L, FFN_HIDDEN, D), FFN_HIDDEN ** -0.5),
    }

def first_block(x, c, ada_w, ada_b, pre1_w, post1_w, pre2_w, post2_w, w_in, gla_a2, gla_a_b,
              gla_norm_w, ml_conv_w, ml_conv_b, ml_i_b, ml_f_b, s5_lam_re, s5_lam_im, s5_log_step,
              s5_b_re, s5_b_im, s5_c_re, s5_c_im, s5_d, s5_glu_w, s5_glu_b, proj_gla, proj_ml,
              proj_s5, branch_gate_b, w_out, ffn_w_in, ffn_w_out):
    c_act = jax.nn.silu(c)
    for l in range(DEPTH):
        mod = c_act @ ada_w[l] + ada_b[l]
        sh1, sc1, gt1, sh2, sc2, gt2 = [m[:, None, :] for m in jnp.split(mod, 6, axis=-1)]

        h = rms_norm(x, pre1_w[l]) * (1.0 + sc1) + sh1
        y = hybrid_mixer(h, w_in[l], gla_a2[l], gla_a_b[l], gla_norm_w[l], ml_conv_w[l], ml_conv_b[l],
                         ml_i_b[l], ml_f_b[l], s5_lam_re[l], s5_lam_im[l], s5_log_step[l],
                         s5_b_re[l], s5_b_im[l], s5_c_re[l], s5_c_im[l], s5_d[l], s5_glu_w[l],
                         s5_glu_b[l], proj_gla[l], proj_ml[l], proj_s5[l], branch_gate_b[l], w_out[l])
        x = x + (1.0 + gt1) * rms_norm(y, post1_w[l])

        h = rms_norm(x, pre2_w[l]) * (1.0 + sc2) + sh2
        y = swiglu_ffn(h, ffn_w_in[l], ffn_w_out[l])
        x = x + (1.0 + gt2) * rms_norm(y, post2_w[l])
    return x


DEPTH_2 = 2

MEM_LEN = 256
HEAD_DIM = 64
N_MIX_HEADS = D_MODEL // HEAD_DIM
N_MEM_HEADS = 4
N_TOK_HEADS = N_MIX_HEADS - N_MEM_HEADS
TOK_WIDTH = N_TOK_HEADS * HEAD_DIM
MEM_WIDTH = N_MEM_HEADS * HEAD_DIM
MIX_WIDTH = TOK_WIDTH + MEM_WIDTH
Q_LORA = 384
KV_LORA = 256
QK_NOPE = 64
QK_ROPE = 32
V_DIM = HEAD_DIM
QK_DIM = QK_NOPE + QK_ROPE
ROPE_THETA = 10000.0
Q_BLOCK = 128
CONV_W = 4
LRU_C = 8.0
N_LRU_BLOCKS = N_TOK_HEADS
LRU_BLOCK = TOK_WIDTH // N_LRU_BLOCKS
ALPHA = (2.0 * DEPTH_2) ** 0.25
BETA = (8.0 * DEPTH_2) ** -0.25
NORM_EPS = 1e-6
N_MLA = (DEPTH_2 + 1) // 2
N_LRU = DEPTH_2 // 2
MLA_IN = Q_LORA + KV_LORA + QK_ROPE + MIX_WIDTH + MEM_WIDTH
LRU_IN = TOK_WIDTH + MIX_WIDTH + MEM_WIDTH


def _split_2(t, sizes):
    idx = np.cumsum(sizes)[:-1].tolist()
    return jnp.split(t, idx, axis=-1)

def rms_norm_2(t, g):
    t32 = t.astype(jnp.float32)
    t32 = t32 * lax.rsqrt(jnp.mean(t32 * t32, axis=-1, keepdims=True) + NORM_EPS)
    return (t32 * g.astype(jnp.float32)).astype(t.dtype)

def layer_norm(t, g, b):
    t32 = t.astype(jnp.float32)
    mu = jnp.mean(t32, axis=-1, keepdims=True)
    var = jnp.mean(jnp.square(t32 - mu), axis=-1, keepdims=True)
    y = (t32 - mu) * lax.rsqrt(var + NORM_EPS)
    return (y * g.astype(jnp.float32) + b.astype(jnp.float32)).astype(t.dtype)

def apply_rope(t, positions):
    half = t.shape[-1] // 2
    inv_freq = ROPE_THETA ** (-jnp.arange(half, dtype=jnp.float32) / half)
    ang = positions.astype(jnp.float32)[..., None] * inv_freq
    cos = jnp.cos(ang)[:, :, None, :].astype(t.dtype)
    sin = jnp.sin(ang)[:, :, None, :].astype(t.dtype)
    t1, t2 = t[..., :half], t[..., half:]
    return jnp.concatenate([t1 * cos - t2 * sin, t1 * sin + t2 * cos], axis=-1)

def causal_attention(q, k, v):
    b, s, h, d = q.shape
    nb = s // Q_BLOCK
    scale = 1.0 / math.sqrt(d)
    qb = q.reshape(b, nb, Q_BLOCK, h, d).transpose(1, 0, 2, 3, 4)
    k_pos = jnp.arange(s)

    def one_block(args):
        q_blk, blk = args
        sc = jnp.einsum('bqhd,bkhd->bhqk', q_blk, k,
                        preferred_element_type=jnp.float32) * scale
        q_pos = blk * Q_BLOCK + jnp.arange(Q_BLOCK)
        mask = k_pos[None, :] <= q_pos[:, None]
        sc = jnp.where(mask[None, None], sc, -jnp.inf)
        p = jax.nn.softmax(sc, axis=-1).astype(v.dtype)
        return jnp.einsum('bhqk,bkhd->bqhd', p, v)

    out = lax.map(one_block, (qb, jnp.arange(nb)))
    return out.transpose(1, 0, 2, 3, 4).reshape(b, s, h, v.shape[-1])

def memory_attention(q, mem_k, mem_v):
    sc = jnp.einsum('bshd,bmhd->bhsm', q, mem_k,
                    preferred_element_type=jnp.float32) / math.sqrt(HEAD_DIM)
    p = jax.nn.softmax(sc, axis=-1).astype(mem_v.dtype)
    return jnp.einsum('bhsm,bmhd->bshd', p, mem_v)

def _lin_rec_combine(left, right):
    a1, b1 = left
    a2, b2 = right
    return a1 * a2, a2 * b1 + b2

def rg_lru_branch(u, conv_w, conv_b, w_r, b_r, w_i, b_i, lam):
    b, s, w = u.shape
    u_pad = jnp.pad(u, ((0, 0), (CONV_W - 1, 0), (0, 0)))
    xc = conv_b + u_pad[:, 0:s] * conv_w[0]
    for tap in range(1, CONV_W):
        xc = xc + u_pad[:, tap:tap + s] * conv_w[tap]
    xb = xc.reshape(b, s, N_LRU_BLOCKS, LRU_BLOCK)
    r = jax.nn.sigmoid(jnp.einsum('bsgi,gij->bsgj', xb, w_r).reshape(b, s, w) + b_r)
    i = jax.nn.sigmoid(jnp.einsum('bsgi,gij->bsgj', xb, w_i).reshape(b, s, w) + b_i)
    log_a = (-LRU_C * jax.nn.softplus(-lam.astype(jnp.float32))) * r.astype(jnp.float32)
    a = jnp.exp(log_a)
    gated_x = jnp.sqrt(-jnp.expm1(2.0 * log_a)) * (i * xc).astype(jnp.float32)
    _, hs = lax.associative_scan(_lin_rec_combine, (a, gated_x), axis=1)
    return hs.astype(u.dtype)

def second_inputs(seed: int = 0) -> dict:
    key = jax.random.key(seed)
    ks = jax.random.split(key, 24)
    f32 = jnp.float32
    nrm = lambda k, shape, s: jax.random.normal(k, shape, f32) * s
    x = nrm(ks[0], (BATCH, SEQ, D_MODEL), 1.0)
    mem = nrm(ks[1], (BATCH, MEM_LEN, D_MODEL), 1.0)
    offset = jax.random.randint(ks[2], (BATCH, 1), 0, 4096, dtype=jnp.int32)
    positions = (offset + jnp.arange(SEQ, dtype=jnp.int32)[None, :]).astype(jnp.int32)
    mla_w_in = nrm(ks[3], (N_MLA, D_MODEL, MLA_IN), D_MODEL ** -0.5)
    mla_q_norm = 1.0 + nrm(ks[4], (N_MLA, Q_LORA), 0.01)
    mla_w_uq = nrm(ks[5], (N_MLA, Q_LORA, N_TOK_HEADS * QK_DIM), Q_LORA ** -0.5)
    mla_kv_norm = 1.0 + nrm(ks[6], (N_MLA, KV_LORA), 0.01)
    mla_w_ukv = nrm(ks[7], (N_MLA, KV_LORA, N_TOK_HEADS * (QK_NOPE + V_DIM)), KV_LORA ** -0.5)
    lru_w_in = nrm(ks[8], (N_LRU, D_MODEL, LRU_IN), D_MODEL ** -0.5)
    lru_conv_w = nrm(ks[9], (N_LRU, CONV_W, TOK_WIDTH), CONV_W ** -0.5)
    lru_conv_b = nrm(ks[10], (N_LRU, TOK_WIDTH), 0.01)
    lru_w_rgate = nrm(ks[11], (N_LRU, N_LRU_BLOCKS, LRU_BLOCK, LRU_BLOCK), LRU_BLOCK ** -0.5)
    lru_b_rgate = nrm(ks[12], (N_LRU, TOK_WIDTH), 0.01)
    lru_w_igate = nrm(ks[13], (N_LRU, N_LRU_BLOCKS, LRU_BLOCK, LRU_BLOCK), LRU_BLOCK ** -0.5)
    lru_b_igate = nrm(ks[14], (N_LRU, TOK_WIDTH), 0.01)
    a_c = jax.random.uniform(ks[15], (N_LRU, TOK_WIDTH), f32, 0.9, 0.999)
    a0 = a_c ** (1.0 / LRU_C)
    lru_lambda = jnp.log(a0) - jnp.log1p(-a0)
    w_mem_kv = nrm(ks[16], (DEPTH_2, D_MODEL, 2 * MEM_WIDTH), D_MODEL ** -0.5)
    w_out = nrm(ks[17], (DEPTH_2, MIX_WIDTH, D_MODEL), BETA * MIX_WIDTH ** -0.5)
    ln_g = 1.0 + nrm(ks[18], (DEPTH_2, D_MODEL), 0.01)
    ln_b = nrm(ks[19], (DEPTH_2, D_MODEL), 0.01)
    return {"x": x, "mem": mem, "positions": positions,
            "mla_w_in": mla_w_in, "mla_q_norm": mla_q_norm, "mla_w_uq": mla_w_uq,
            "mla_kv_norm": mla_kv_norm, "mla_w_ukv": mla_w_ukv,
            "lru_w_in": lru_w_in, "lru_conv_w": lru_conv_w, "lru_conv_b": lru_conv_b,
            "lru_w_rgate": lru_w_rgate, "lru_b_rgate": lru_b_rgate,
            "lru_w_igate": lru_w_igate, "lru_b_igate": lru_b_igate, "lru_lambda": lru_lambda,
            "w_mem_kv": w_mem_kv, "w_out": w_out, "ln_g": ln_g, "ln_b": ln_b}

def second_block(x, mem, positions, mla_w_in, mla_q_norm, mla_w_uq, mla_kv_norm, mla_w_ukv,
              lru_w_in, lru_conv_w, lru_conv_b, lru_w_rgate, lru_b_rgate,
              lru_w_igate, lru_b_igate, lru_lambda, w_mem_kv, w_out, ln_g, ln_b):
    b, s, _ = x.shape
    h = x
    for layer in range(DEPTH_2):
        j = layer // 2
        if layer % 2 == 0:
            z = h @ mla_w_in[j]
            c_q, c_kv, k_r, gate, q_mem = _split_2(
                z, [Q_LORA, KV_LORA, QK_ROPE, MIX_WIDTH, MEM_WIDTH])
            q = (rms_norm_2(c_q, mla_q_norm[j]) @ mla_w_uq[j]).reshape(b, s, N_TOK_HEADS, QK_DIM)
            q = jnp.concatenate([q[..., :QK_NOPE], apply_rope(q[..., QK_NOPE:], positions)], axis=-1)
            kv = (rms_norm_2(c_kv, mla_kv_norm[j]) @ mla_w_ukv[j]).reshape(
                b, s, N_TOK_HEADS, QK_NOPE + V_DIM)
            k_nope, v = kv[..., :QK_NOPE], kv[..., QK_NOPE:]
            k_rope = apply_rope(k_r[:, :, None, :], positions)
            k = jnp.concatenate(
                [k_nope, jnp.broadcast_to(k_rope, (b, s, N_TOK_HEADS, QK_ROPE))], axis=-1)
            tok = causal_attention(q, k, v).reshape(b, s, TOK_WIDTH)
        else:
            z = h @ lru_w_in[j]
            u, gate, q_mem = _split_2(z, [TOK_WIDTH, MIX_WIDTH, MEM_WIDTH])
            tok = rg_lru_branch(u, lru_conv_w[j], lru_conv_b[j], lru_w_rgate[j], lru_b_rgate[j],
                                lru_w_igate[j], lru_b_igate[j], lru_lambda[j])
        mem_kv = (mem @ w_mem_kv[layer]).reshape(b, MEM_LEN, 2, N_MEM_HEADS, HEAD_DIM)
        mem_out = memory_attention(q_mem.reshape(b, s, N_MEM_HEADS, HEAD_DIM),
                                   mem_kv[:, :, 0], mem_kv[:, :, 1]).reshape(b, s, MEM_WIDTH)
        y = jnp.concatenate([tok, mem_out], axis=-1) * jax.nn.silu(gate)
        h = layer_norm(ALPHA * h + y @ w_out[layer], ln_g[layer], ln_b[layer])
    return h


def setup_inputs(seed=0):
    out = dict(first_inputs(seed))
    for name, value in second_inputs(seed + 1).items():
        if name != "x":
            out[name + "_2"] = value
    return out


def reference(
    x, c, ada_w, ada_b, pre1_w, post1_w, pre2_w, post2_w, w_in, gla_a2, gla_a_b, gla_norm_w,
    ml_conv_w, ml_conv_b, ml_i_b, ml_f_b, s5_lam_re, s5_lam_im, s5_log_step, s5_b_re, s5_b_im,
    s5_c_re, s5_c_im, s5_d, s5_glu_w, s5_glu_b, proj_gla, proj_ml, proj_s5, branch_gate_b,
    w_out, ffn_w_in, ffn_w_out, mem_2, positions_2, mla_w_in_2, mla_q_norm_2, mla_w_uq_2,
    mla_kv_norm_2, mla_w_ukv_2, lru_w_in_2, lru_conv_w_2, lru_conv_b_2, lru_w_rgate_2,
    lru_b_rgate_2, lru_w_igate_2, lru_b_igate_2, lru_lambda_2, w_mem_kv_2, w_out_2, ln_g_2,
    ln_b_2,
):
    x = first_block(
        x, c, ada_w, ada_b, pre1_w, post1_w, pre2_w, post2_w, w_in, gla_a2, gla_a_b, gla_norm_w,
        ml_conv_w, ml_conv_b, ml_i_b, ml_f_b, s5_lam_re, s5_lam_im, s5_log_step, s5_b_re,
        s5_b_im, s5_c_re, s5_c_im, s5_d, s5_glu_w, s5_glu_b, proj_gla, proj_ml, proj_s5,
        branch_gate_b, w_out, ffn_w_in, ffn_w_out,
    )
    return second_block(
        x, mem_2, positions_2, mla_w_in_2, mla_q_norm_2, mla_w_uq_2, mla_kv_norm_2, mla_w_ukv_2,
        lru_w_in_2, lru_conv_w_2, lru_conv_b_2, lru_w_rgate_2, lru_b_rgate_2, lru_w_igate_2,
        lru_b_igate_2, lru_lambda_2, w_mem_kv_2, w_out_2, ln_g_2, ln_b_2,
    )


_drawn_inputs = setup_inputs


def setup_inputs(seed=0):
    import zlib

    import numpy as np

    out = dict(_drawn_inputs(seed))
    spreads = {}
    factors = {'ml_conv_b': 6.677,
     'ml_i_b': 7.322,
     's5_lam_re': 200.0,
     's5_glu_b': 8.0,
     'branch_gate_b': 8.0,
     'mla_q_norm_2': 8.0,
     'mla_kv_norm_2': 8.0,
     'lru_conv_b_2': 20.096,
     'lru_b_rgate_2': 64.0,
     'lru_b_igate_2': 56.961,
     'ln_g_2': 40.268,
     'ln_b_2': 21.52}
    for name, (base, spread) in spreads.items():
        noise = np.random.default_rng([zlib.crc32(name.encode()), seed]).standard_normal(out[name].shape)
        drawn = base * np.exp(spread * noise) if base else spread * noise
        out[name] = jnp.asarray(drawn.astype(out[name].dtype))
    for name, factor in factors.items():
        out[name] = (out[name] * factor).astype(out[name].dtype)
    return out
```

```python
import math
from contextlib import ExitStack

import numpy as np

import concourse.bass as bass
from concourse import mybir

F32 = mybir.dt.float32
I32 = mybir.dt.int32
ACT = mybir.ActivationFunctionType
ALU = mybir.AluOpType
AX = mybir.AxisListType

P = 128
D = 1024
T = 1024
DT = D // P
HALF = 512
CH = T // P
RING = 4
SLOT = 8
HEADS = 4
DK = 64
FFN = 2816
FT = FFN // P
TOK_HEADS = 12
MEM_HEADS = 4
MEM = 256
QK = 96
EPS = 1e-6
ALPHA = 4.0 ** 0.25
BIG = float(2.0 ** 100)
TWO_PI = 2.0 * math.pi
MAGIC = 12582912.0

VEC = {}


def _columns():
    at = 0
    for name, n in [("c", 8), ("ada_b", 48), ("pre1_w", 8), ("post1_w", 8), ("pre2_w", 8), ("post2_w", 8),
                    ("gla_a_b", 2), ("gla_norm_w", 4), ("conv_w", 16), ("conv_b", 4), ("s5_d", 4),
                    ("glu_b", 4), ("gate_b", 24), ("lam_re", 16), ("lam_im", 16), ("log_step", 16),
                    ("q_norm", 3), ("kv_norm", 2), ("lru_conv_w", 24), ("lru_conv_b", 6), ("b_r", 6),
                    ("b_i", 6), ("lam", 6), ("ln_g", 16), ("ln_b", 16), ("i_b", 1), ("f_b", 1),
                    ("inv_freq", 1), ("rope_sign", 1)]:
        VEC[name] = (at, n)
        at += n
    return at


NVEC = _columns()

CONST = {}


def _constants():
    at = 0
    for name, n in [("ident", P), ("ones", P), ("mask_qk", P), ("mask_kq", P), ("diag", P), ("sel", HEADS * P),
                    ("ramp", 32)]:
        CONST[name] = (at, n)
        at += n
    return at


NCONST = _constants()


class Count:

    def __init__(self, sem):
        self.sem, self.n = sem, 0


class Link:

    def __init__(self, eng, count):
        self.eng, self.count, self.k, self.i, self.per = eng, count, 0, None, 0

    def loop(self, i, per):
        self.i, self.per, self.k = i, per, 0

    def __call__(self, ins):
        self.k += 1
        ins.then_inc(self.count.sem, 1)
        value = self.count.n + self.k
        if self.i is not None:
            value = self.i * self.per + value
        self.eng.wait_ge(self.count.sem, value)

    def close(self, iters=1):
        if self.i is not None:
            assert self.k == self.per, (self.k, self.per)
        self.count.n += self.k * iters


def build(nc, a):
    ctx = ExitStack()
    with ctx:
        names = {}

        def sb_in(scope, name, shape, dt=F32):
            names[name] = names.get(name, 0) + 1
            name = f"{name}_sb{names[name]}"
            return scope.enter_context(nc.sbuf_tensor(name, shape, dt))

        def sb(name, shape, dt=F32):
            return sb_in(ctx, name, shape, dt)

        def sem(name):
            return Count(ctx.enter_context(nc.semaphore(name)))

        ps = ctx.enter_context(nc.psum_tensor("ps", [P, 8, HALF], F32))
        pair = [ps[:, 2 * p:2 * p + 2, :].rearrange("p a n -> p (a n)") for p in range(4)]

        ring = sb("ring", [P, RING, SLOT, P])
        vec = sb("vec", [P, NVEC])
        cst = sb("cst", [P, NCONST])
        mod = sb("mod", [P, 48])
        fold = sb("fold", [P, 32])
        act0 = sb("act0", [P, 8])
        H = sb("H", [P, DT, T])

        def V(name, j=0, n=1):
            at = VEC[name][0]
            return vec[:, at + j:at + j + n]

        def C(name, lo=0, hi=None):
            at, n = CONST[name]
            return cst[:, at + lo:at + (n if hi is None else hi)]

        ident, ones = C("ident"), C("ones")

        w_full = [sem(f"w_full{s}") for s in range(RING)]
        pe_done = sem("pe_done")
        act_free = sem("act_free")
        dve_free = sem("dve_free")
        act_own = sem("act_own")
        dve_own = sem("dve_own")
        pool_own = sem("pool_own")
        loaded = sem("loaded")
        stored = sem("stored")
        act_out = sem("act_out")
        dve_out = sem("dve_out")
        pool_out = sem("pool_out")
        pe_s, pe_o, act_p, dve_o = sem("pe_s"), sem("pe_o"), sem("act_p"), sem("dve_o")
        free = {"act": act_free, "dve": dve_free}
        stream = {"slot": 0}
        n_slots = a["w"].shape[0]

        def refill(sp, i, s0, per_body, released, base, per_turn=None):
            for sl in range(per_body):
                n = s0 + sl + RING
                if i is None and n >= n_slots:
                    return
                value = base + released[sl]
                if i is not None:
                    value = i * (per_turn or released[-1]) + value
                    src = a["w"][i * per_body + n]
                else:
                    src = a["w"][n]
                sp.wait_ge(pe_done.sem, value)
                sp.dma_start(ring[:, n % RING].rearrange("p t m -> p (t m)"), src).then_inc(w_full[n % RING].sem, 16)

        def linear(nm, kt, rhs, plan, emit, ktp=None, own=None, ntok=T, mcols=None):
            ktp = ktp or kt
            U = len(plan)
            iters = nm // U
            assert iters * U == nm
            tiles = U * ktp
            slots = -(-tiles // SLOT)
            if iters > 1:
                assert tiles % SLOT == 0 and slots % RING == 0 and U % 4 == 0
            s0, base = stream["slot"], pe_done.n
            halves = -(-ntok // HALF)
            events, job_at, slot_at = 0, {}, {}
            marks = {}
            for u in range(U):
                for k in range(kt):
                    t = u * ktp + k
                    last_of_slot = t // SLOT != (t + 1) // SLOT or k == kt - 1 and (
                        (u + 1) * ktp // SLOT != t // SLOT) or (u == U - 1 and k == kt - 1)
                    if k == kt - 1 or last_of_slot:
                        events += 1
                        marks[(u, k)] = events
                        if k == kt - 1:
                            job_at[u] = events
                        if last_of_slot:
                            slot_at[t // SLOT] = events
            released = [slot_at[s] for s in range(slots)]
            released_all = released[:-1] + [events] if released[-1] != events else released
            assert released_all[-1] == events
            order = {e: [u for u in range(U) if plan[u] == e] for e in ("act", "dve")}

            with nc.Block() as block:
                @block.sync
                def _(sp):
                    if iters == 1:
                        refill(sp, None, s0, slots, released_all, base)
                    else:
                        with sp.Fori(0, iters, 1) as i:
                            refill(sp, i, s0, slots, released_all, base)

                @block.tensor
                def _(pe):
                    def body(i):
                        for u in range(U):
                            if i is not None or u >= 4:
                                before = (u - 4) % U
                                e = plan[before]
                                mine = order[e]
                                value = free[e].n + mine.index(before) + 1 - (len(mine) if u < 4 else 0)
                                if i is not None:
                                    assert value >= 0
                                    value = i * len(mine) + value
                                pe.wait_ge(free[e].sem, value)
                            for k in range(kt):
                                t = u * ktp + k
                                n = s0 + t // SLOT
                                if t % SLOT == 0 or (k == 0 and t // SLOT != (t - 1) // SLOT):
                                    value = 16 * (n // RING + 1)
                                    if i is not None:
                                        value = i * (16 * slots // RING) + value
                                    pe.wait_ge(w_full[n % RING].sem, value)
                                w = ring[:, n % RING, t % SLOT, :]
                                for h in range(halves):
                                    width = min(HALF, ntok)
                                    mm = nc.tensor.matmul(pair[u % 4][:, h * HALF:h * HALF + width], w, rhs(u, k, h),
                                                          start=(k == 0), stop=(k == kt - 1))
                                if (u, k) in marks:
                                    mm.then_inc(pe_done.sem, 1)
                    if iters == 1:
                        body(None)
                    else:
                        with pe.Fori(0, iters, 1) as i:
                            body(i)

                def evacuate(e, eng):
                    if not order[e]:
                        return
                    link = Link(eng, act_own if e == "act" else dve_own)

                    def body(i):
                        if i is not None:
                            link.loop(i, (own or {}).get(e, 0))
                        for u in order[e]:
                            value = base + job_at[u]
                            m = u
                            if i is not None:
                                value = i * events + value
                                m = i * U + u
                            eng.wait_ge(pe_done.sem, value)
                            emit(e, link, m, u, pair[u % 4][:, 0:ntok], i).then_inc(free[e].sem, 1)
                    if iters == 1:
                        body(None)
                    else:
                        with eng.Fori(0, iters, 1) as i:
                            body(i)
                    link.close(iters)

                @block.scalar
                def _(act):
                    evacuate("act", act)

                @block.vector
                def _(dve):
                    evacuate("dve", dve)
            pe_done.n += events * iters
            for e in order:
                free[e].n += len(order[e]) * iters
            stream["slot"] += slots * iters

        def token_major(chunks, cols, kt, lhs, dest):
            per = SLOT * P // cols
            slots = kt // per
            s0, base = stream["slot"], pe_done.n
            with nc.Block() as block:
                @block.sync
                def _(sp):
                    refill(sp, None, s0, slots, [s + 1 for s in range(slots - 1)] + [slots - 1 + chunks], base)

                @block.tensor
                def _(pe):
                    for k in range(kt):
                        n = s0 + k // per
                        if k % per == 0:
                            pe.wait_ge(w_full[n % RING].sem, 16 * (n // RING + 1))
                        w = ring[:, n % RING].rearrange("p t m -> p (t m)")[:, (k % per) * cols:(k % per + 1) * cols]
                        for c in range(chunks):
                            mm = nc.tensor.matmul(ps[:, c, 0:cols], lhs(k, c), w, start=(k == 0), stop=(k == kt - 1))
                            if k == kt - 1:
                                mm.then_inc(pe_done.sem, 1)
                        if k % per == per - 1 and k != kt - 1:
                            mm.then_inc(pe_done.sem, 1)

                @block.scalar
                def _(act):
                    for c in range(0, chunks, 2):
                        act.wait_ge(pe_done.sem, base + slots - 1 + c + 1)
                        dest(c, lambda out, src: nc.scalar.activation(out, src, ACT.Copy), ps[:, c, 0:cols])

                @block.vector
                def _(dve):
                    for c in range(1, chunks, 2):
                        dve.wait_ge(pe_done.sem, base + slots - 1 + c + 1)
                        dest(c, nc.vector.tensor_copy, ps[:, c, 0:cols])
            pe_done.n += slots - 1 + chunks
            stream["slot"] += slots

        def norm(src, n, groups, width, scale, out, bias=None, residual=None, gate=None, center=None):
            per = n // groups
            with ExitStack() as scope:
                sq = sb_in(scope, "norm_sq", [P, 2, T])
                rstd = sb_in(scope, "norm_rstd", [P, 2, T])
                base, b_act, b_dve, b_out = pe_done.n, act_out.n, dve_out.n, dve_free.n
                with nc.Block() as block:
                    @block.scalar
                    def _(act):
                        for t in range(n):
                            if t >= 2:
                                act.wait_ge(pe_done.sem, base + t - 1)
                            if center is not None:
                                act.wait_ge(dve_out.sem, b_dve + t + 1)
                            nc.scalar.activation(sq[:, t % 2], src(t), ACT.Square).then_inc(act_out.sem, 1)
                        for g in range(groups):
                            act.wait_ge(dve_free.sem, b_out + g + 1)
                            nc.scalar.activation(rstd[:, g % 2], rstd[:, g % 2], ACT.Sqrt).then_inc(act_out.sem, 1)

                    @block.tensor
                    def _(pe):
                        for t in range(n):
                            pe.wait_ge(act_out.sem, b_act + t + 1)
                            for h in range(2):
                                mm = nc.tensor.matmul(pair[t // per][:, h * HALF:(h + 1) * HALF], ones,
                                                      sq[:, t % 2, h * HALF:(h + 1) * HALF],
                                                      start=(t % per == 0), stop=(t % per == per - 1))
                            mm.then_inc(pe_done.sem, 1)

                    @block.vector
                    def _(dve):
                        link = Link(dve, dve_own)
                        if center is not None:
                            for t in range(n):
                                nc.vector.tensor_tensor(src(t), src(t), center, ALU.subtract).then_inc(dve_out.sem, 1)
                        for g in range(groups):
                            dve.wait_ge(pe_done.sem, base + (g + 1) * per)
                            link(nc.vector.tensor_scalar(rstd[:, g % 2], pair[g], 1.0 / width, EPS, ALU.mult, ALU.add))
                            nc.vector.reciprocal(rstd[:, g % 2], rstd[:, g % 2]).then_inc(dve_free.sem, 1)
                            dve.wait_ge(act_out.sem, b_act + n + g + 1)
                            for t in range(g * per, (g + 1) * per):
                                link(nc.vector.scalar_tensor_tensor(out(t), src(t), scale(t), rstd[:, g % 2],
                                                                    ALU.mult, ALU.mult))
                                if bias is not None:
                                    link(nc.vector.tensor_scalar(out(t), out(t), bias(t), None, ALU.add))
                                if residual is not None:
                                    link(nc.vector.tensor_tensor(out(t), out(t), residual(t), ALU.add))
                                if gate is not None:
                                    link(nc.vector.tensor_tensor(out(t), out(t), gate(t), ALU.mult))
                        link.close()
                pe_done.n += n
                act_out.n += n + groups
                dve_free.n += groups
                if center is not None:
                    dve_out.n += n

        def load(dst, src):
            with nc.Block() as block:
                @block.sync
                def _(sp):
                    sp.dma_start(dst, src).then_inc(loaded.sem, 16)
                    loaded.n += 16
                    sp.wait_ge(loaded.sem, loaded.n)

        with nc.Block() as block:
            @block.sync
            def _(sp):
                sp.dma_start(vec[:], a["vec"]).then_inc(loaded.sem, 16)
                sp.dma_start(cst[:], a["cst"]).then_inc(loaded.sem, 16)
                loaded.n += 32
                for n in range(RING):
                    sp.dma_start(ring[:, n].rearrange("p t m -> p (t m)"), a["w"][n]).then_inc(w_full[n].sem, 16)

            @block.scalar
            def _(act):
                act.wait_ge(loaded.sem, 32)
                nc.scalar.activation(act0[:], V("c", 0, 8), ACT.Silu)

        ADA_BODY = 4
        ada_iters = 48 // ADA_BODY
        s0, base = stream["slot"], pe_done.n
        with nc.Block() as block:
            @block.sync
            def _(sp):
                with sp.Fori(0, ada_iters, 1) as i:
                    refill(sp, i, s0, ADA_BODY, [1, 2, 3, 4], base)

            @block.tensor
            def _(pe):
                with pe.Fori(0, ada_iters, 1) as i:
                    for u in range(ADA_BODY):
                        pe.wait_ge(w_full[u].sem, i * 16 + 16)
                        for k in range(DT):
                            mm = nc.tensor.matmul(ps[:, 0, bass.ds(i * ADA_BODY + u, 1)], ring[:, u, k, :],
                                                  act0[:, k:k + 1], start=(k == 0), stop=(k == DT - 1))
                        mm.then_inc(pe_done.sem, 1)

            @block.vector
            def _(dve):
                link = Link(dve, dve_own)
                dve.wait_ge(pe_done.sem, base + 48)
                link(nc.vector.tensor_tensor(mod[:], ps[:, 0, 0:48], V("ada_b", 0, 48), ALU.add))
                for j, (w, m) in enumerate([("pre1_w", 8), ("post1_w", 16), ("pre2_w", 32), ("post2_w", 40)]):
                    link(nc.vector.scalar_tensor_tensor(fold[:, 8 * j:8 * j + 8], mod[:, m:m + 8], 1.0, V(w, 0, 8),
                                                        ALU.add, ALU.mult))
                nc.vector.memset(act0[:, 0:1], 0.0).then_inc(dve_free.sem, 8)
                dve_free.n += 8
                link.close()

            @block.scalar
            def _(act):
                act.wait_ge(pe_done.sem, base + 48)
                nc.scalar.activation(act0[:, 1:2], act0[:, 1:2], ACT.Copy).then_inc(act_free.sem, 8)
                act_free.n += 8
        pe_done.n += 48
        stream["slot"] += 48

        with ExitStack() as scope:
            x0 = sb_in(scope, "x0", [P, DT, T])
            load(x0[:], a["x"])
            norm(lambda t: x0[:, t], DT, 1, D, lambda t: fold[:, t:t + 1], lambda t: H[:, t],
                 bias=lambda t: mod[:, t:t + 1])

        def from_h(u, k, h):
            return H[:, k, h * HALF:(h + 1) * HALF]

        def copy_to(dest):
            def emit(e, link, m, u, src, i):
                if e == "act":
                    return nc.scalar.activation(dest(m), src, ACT.Copy)
                return nc.vector.tensor_copy(dest(m), src)
            return emit

        def act_to(dest, func, bias=None, scale=1.0):
            def emit(e, link, m, u, src, i):
                return nc.scalar.activation(dest(m), src, func, bias=bias(m) if bias else 0.0, scale=scale)
            return emit

        Y = sb("Y", [P, 4, T])
        small = sb("small", [HEADS, 2, T])

        with ExitStack() as scope:
            q = sb_in(scope, "gla_q", [P, 2, T])
            k_ = sb_in(scope, "gla_k", [P, 2, T])
            v = sb_in(scope, "gla_v", [P, CH, 4 * P])
            cum = sb_in(scope, "gla_cum", [P, 2, T])
            sc = sb_in(scope, "gla_scores", [P, CH, 4 * P])
            with ExitStack() as s2:
                ga = sb_in(s2, "gla_ga", [16, T])

                def emit(e, link, m, u, src, i):
                    if u < 2:
                        return nc.scalar.activation(q[:, u], src, ACT.Copy, scale=DK ** -0.5)
                    if u < 4:
                        return nc.vector.tensor_copy(k_[:, u - 2], src)
                    nc.scalar.activation(ga[:], src[0:16], ACT.Copy)
                    nc.scalar.activation(small[:, 0], src[32:36], ACT.Copy)
                    return nc.scalar.activation(small[:, 1], src[64:68], ACT.Copy)
                linear(5, 8, from_h, ["act", "act", "dve", "dve", "act"], emit)
                token_major(CH, 4 * P, DT, lambda k, c: H[:, k, c * P:(c + 1) * P], lambda c, op, src: op(v[:, c], src))

                z = sb_in(s2, "gla_z", [P, 2, T])
                t1 = sb_in(s2, "gla_t1", [P, 2, T])
                reset = sb_in(s2, "gla_reset", [P, 2, T])
                a2 = sb_in(s2, "gla_a2", [16, 2 * P])
                load(a2[:], a["gla_a2"])
                base, b_act, b_dve = pe_done.n, act_out.n, dve_out.n
                with nc.Block() as block:
                    @block.tensor
                    def _(pe):
                        for m in range(2):
                            for h in range(2):
                                mm = nc.tensor.matmul(pair[m][:, h * HALF:(h + 1) * HALF], a2[:, m * P:(m + 1) * P],
                                                      ga[:, h * HALF:(h + 1) * HALF], start=True, stop=True)
                            mm.then_inc(pe_done.sem, 1)

                    @block.scalar
                    def _(act):
                        for m in range(2):
                            act.wait_ge(dve_out.sem, b_dve + m + 1)
                            nc.scalar.activation(t1[:, m], t1[:, m], ACT.Exp, scale=-1.0).then_inc(act_own.sem, 1)
                            act.wait_ge(act_own.sem, act_own.n + m + 1)
                            nc.scalar.activation(t1[:, m], t1[:, m], ACT.Ln, bias=1.0).then_inc(act_out.sem, 1)
                        act_own.n += 2

                    @block.vector
                    def _(dve):
                        link = Link(dve, dve_own)
                        link(nc.vector.memset(reset[:], 1.0))
                        link(nc.vector.memset(reset[:].rearrange("p a (c j) -> p (a c) j", j=P)[:, :, 0:1], 0.0))
                        for m in range(2):
                            dve.wait_ge(pe_done.sem, base + m + 1)
                            link(nc.vector.tensor_scalar(z[:, m], pair[m], V("gla_a_b", m), None, ALU.add))
                            nc.vector.scalar_tensor_tensor(t1[:, m], z[:, m], -1.0, z[:, m], ALU.mult,
                                                           ALU.max).then_inc(dve_out.sem, 1)
                        for m in range(2):
                            dve.wait_ge(act_out.sem, b_act + m + 1)
                            link(nc.vector.scalar_tensor_tensor(z[:, m], z[:, m], 0.0, t1[:, m], ALU.min, ALU.subtract))
                            link(nc.vector.tensor_scalar(z[:, m], z[:, m], 1.0 / 16.0, None, ALU.mult))
                            link(nc.vector.tensor_tensor_scan(cum[:, m], reset[:, m], z[:, m], 0.0, ALU.mult, ALU.add))
                        link.close()
                pe_done.n += 2
                act_out.n += 2
                dve_out.n += 2

            with ExitStack() as s2:
                masks = sb_in(s2, "gla_masks", [P, 7, P], I32)
                delta = sb_in(s2, "gla_delta", [P, 2 * T])
                decay = sb_in(s2, "gla_decay", [P, 2 * T])
                qe = sb_in(s2, "gla_qe", [P, 2, T])
                ke = sb_in(s2, "gla_ke", [P, 2, T])
                load(masks[:], a["masks"])
                flat_cum = cum[:].rearrange("p a n -> p (a n)")
                flat = lambda ap: ap.rearrange("p a n -> p (a n)")
                base, b_act, b_dve, b_free, b_pool = pe_done.n, act_out.n, dve_out.n, dve_free.n, pool_out.n
                with nc.Block() as block:
                    @block.tensor
                    def _(pe):
                        for lev in range(-1, 7):
                            qs, ks = (q, k_) if lev < 0 else (qe, ke)
                            if lev >= 0:
                                pe.wait_ge(dve_out.sem, b_dve + 2 * (lev + 1))
                                pe.wait_ge(pool_out.sem, b_pool + lev + 1)
                            for c2 in range(CH // 2):
                                if lev >= 0:
                                    pe.wait_ge(dve_free.sem, b_free + CH * lev + 2 * c2 + 2)
                                for j in range(4):
                                    for half in range(2):
                                        h, c = 2 * (j % 2) + half, 2 * c2 + j // 2
                                        r = slice(64 * half, 64 * half + 64)
                                        cols = slice(c * P, (c + 1) * P)
                                        mm = nc.tensor.matmul(ps[:, 2 * c2 + half, j * P:(j + 1) * P],
                                                              ks[r, h // 2, cols], qs[r, h // 2, cols],
                                                              start=True, stop=True)
                                        if j == 3:
                                            mm.then_inc(pe_done.sem, 1)

                    @block.scalar
                    def _(act):
                        for lev in range(7):
                            act.wait_ge(dve_out.sem, b_dve + 2 * lev + 1)
                            if lev > 0:
                                act.wait_ge(pool_out.sem, b_pool + lev)
                                act.wait_ge(dve_out.sem, b_dve + 2 * lev)
                            nc.scalar.activation(decay[:], delta[:], ACT.Abs).then_inc(act_own.sem, 1)
                            act.wait_ge(act_own.sem, act_own.n + lev + 1)
                            nc.scalar.activation(decay[:], decay[:], ACT.Exp, scale=-1.0).then_inc(act_out.sem, 1)
                        act_own.n += 7

                    @block.gpsimd
                    def _(pool):
                        for lev in range(7):
                            pool.wait_ge(act_out.sem, b_act + lev + 1)
                            if lev > 0:
                                pool.wait_ge(pe_done.sem, base + CH * (lev + 1))
                            nc.gpsimd.tensor_tensor(flat(ke[:]), flat(k_[:]), decay[:], ALU.mult).then_inc(pool_out.sem, 1)

                    @block.vector
                    def _(dve):
                        link = Link(dve, dve_own)
                        for lev in range(7):
                            half = 1 << lev
                            blocks = 2 * T // (2 * half)
                            view = lambda ap: ap.rearrange("p (b j) -> p b j", j=2 * half)
                            mid = view(flat_cum)[:, :, half - 1:half].broadcast_to([P, blocks, 2 * half])
                            if lev > 0:
                                dve.wait_ge(act_out.sem, b_act + lev)
                            nc.vector.tensor_tensor(view(delta[:]), view(flat_cum), mid, ALU.subtract
                                                    ).then_inc(dve_out.sem, 1)
                            for c in range(CH):
                                dve.wait_ge(pe_done.sem, base + CH * lev + c + 1)
                                s4 = sc[:, c].rearrange("p (h i) -> p h i", h=HEADS)
                                p4 = ps[:, c].rearrange("p (h i) -> p h i", h=HEADS)
                                if lev == 0:
                                    m4 = C("diag").unsqueeze(1).broadcast_to([P, HEADS, P])
                                    nc.vector.tensor_tensor(s4, p4, m4, ALU.mult).then_inc(dve_free.sem, 1)
                                else:
                                    m4 = masks[:, lev - 1].unsqueeze(1).broadcast_to([P, HEADS, P])
                                    if lev == 1:
                                        dve.wait_ge(dve_free.sem, b_free + c + 1)
                                    nc.vector.copy_predicated(s4, m4, p4).then_inc(dve_free.sem, 1)
                            dve.wait_ge(act_out.sem, b_act + lev + 1)
                            nc.vector.tensor_tensor(flat(qe[:]), flat(q[:]), decay[:], ALU.mult).then_inc(dve_out.sem, 1)
                        for c in range(CH):
                            dve.wait_ge(pe_done.sem, base + CH * 7 + c + 1)
                            m4 = masks[:, 6].unsqueeze(1).broadcast_to([P, HEADS, P])
                            nc.vector.copy_predicated(sc[:, c].rearrange("p (h i) -> p h i", h=HEADS), m4,
                                                      ps[:, c].rearrange("p (h i) -> p h i", h=HEADS)
                                                      ).then_inc(dve_free.sem, 1)
                        link.close()
                pe_done.n += 8 * CH
                act_out.n += 7
                pool_out.n += 7
                dve_out.n += 14
                dve_free.n += 8 * CH

            with ExitStack() as s2:
                e1 = sb_in(s2, "gla_e1", [P, 2 * T])
                e2 = sb_in(s2, "gla_e2", [P, 2 * T])
                last = sb_in(s2, "gla_last", [P, 2 * CH])
                keys = sb_in(s2, "gla_keys", [P, CH, 2, P])
                state = sb_in(s2, "gla_state", [P, CH, 2, P])
                flat_q, flat_k = q[:].rearrange("p a n -> p (a n)"), k_[:].rearrange("p a n -> p (a n)")
                chunked = lambda ap: ap.rearrange("p (b j) -> p b j", j=P)
                base, b_act, b_dve = pe_done.n, act_out.n, dve_out.n
                with nc.Block() as block:
                    @block.scalar
                    def _(act):
                        nc.scalar.activation(e1[:], flat_cum, ACT.Exp).then_inc(act_out.sem, 1)
                        nc.scalar.activation(last[:], chunked(flat_cum)[:, :, P - 1], ACT.Exp).then_inc(act_out.sem, 1)
                        act.wait_ge(dve_out.sem, b_dve + 1)
                        nc.scalar.activation(e2[:], e2[:], ACT.Exp).then_inc(act_out.sem, 1)
                        for c in range(CH // 2):
                            act.wait_ge(pe_done.sem, base + c + 1)
                            nc.scalar.activation(keys[:, 2 * c:2 * c + 2].rearrange("p c a d -> p (c a d)"),
                                                 ps[:, c], ACT.Copy).then_inc(act_out.sem, 1)

                    @block.vector
                    def _(dve):
                        link = Link(dve, dve_own)
                        nc.vector.tensor_tensor(chunked(e2[:]),
                                                chunked(flat_cum)[:, :, P - 1:P].broadcast_to([P, 2 * CH, P]),
                                                chunked(flat_cum), ALU.subtract).then_inc(dve_out.sem, 1)
                        dve.wait_ge(act_out.sem, b_act + 1)
                        nc.vector.tensor_tensor(e1[:], e1[:], flat_q, ALU.mult).then_inc(dve_out.sem, 1)
                        dve.wait_ge(act_out.sem, b_act + 3)
                        nc.vector.tensor_tensor(e2[:], e2[:], flat_k, ALU.mult).then_inc(dve_out.sem, 1)
                        dve.wait_ge(pe_done.sem, base + 5)
                        for a_ in range(2):
                            link(nc.vector.tensor_copy(state[:, 1, a_], ps[:, 4, a_ * P:(a_ + 1) * P]))
                        for c in range(2, CH):
                            for a_ in range(2):
                                at = (c - 1) * 2 + a_
                                ins = nc.vector.scalar_tensor_tensor(
                                    state[:, c, a_], state[:, c - 1, a_], last[:, a_ * CH + c - 1:a_ * CH + c],
                                    ps[:, 4 + at // 4, (at % 4) * P:(at % 4 + 1) * P], ALU.mult, ALU.add)
                                link(ins)
                        nc.vector.memset(state[:, 0], 0.0).then_inc(dve_out.sem, 1)
                        link.close()

                    @block.tensor
                    def _(pe):
                        pe.wait_ge(dve_out.sem, b_dve + 3)
                        for c in range(CH):
                            for a_ in range(2):
                                at = c * 2 + a_
                                mm = nc.tensor.transpose(ps[:, at // 4, (at % 4) * P:(at % 4 + 1) * P],
                                                         e2[:, a_ * T + c * P:a_ * T + (c + 1) * P], ident)
                            if c % 2:
                                mm.then_inc(pe_done.sem, 1)
                        pe.wait_ge(act_out.sem, b_act + 3 + CH // 2)
                        for c in range(CH):
                            for h in range(HEADS):
                                at = c * 2 + h // 2
                                mm = nc.tensor.matmul(
                                    ps[64 * (h % 2):64 * (h % 2) + 64, 4 + at // 4, (at % 4) * P:(at % 4 + 1) * P],
                                    keys[:, c, h // 2, 64 * (h % 2):64 * (h % 2) + 64], v[:, c, h * P:(h + 1) * P],
                                    start=True, stop=True)
                        mm.then_inc(pe_done.sem, 1)
                pe_done.n += CH // 2 + 1
                act_out.n += 3 + CH // 2
                dve_out.n += 4
                base = pe_done.n
                with nc.Block() as block:
                    @block.tensor
                    def _(pe):
                        for h in range(HEADS):
                            r = slice(64 * (h % 2), 64 * (h % 2) + 64)
                            for c in range(CH):
                                o = pair[h][:, c * P:(c + 1) * P]
                                j = 2 * (c % 2) + h // 2
                                mm = nc.tensor.matmul(o, v[:, c, h * P:(h + 1) * P],
                                                      sc[:, 2 * (c // 2) + h % 2, j * P:(j + 1) * P],
                                                      start=True, stop=(c == 0))
                                if c:
                                    mm = nc.tensor.matmul(o, state[r, c, h // 2], e1[r, (h // 2) * T + c * P:
                                                                                     (h // 2) * T + (c + 1) * P],
                                                          start=False, stop=True)
                            mm.then_inc(pe_done.sem, 1)

                    @block.scalar
                    def _(act):
                        for h in range(HEADS):
                            act.wait_ge(pe_done.sem, base + h + 1)
                            nc.scalar.activation(Y[:, h], pair[h], ACT.Copy)
                pe_done.n += HEADS
        with ExitStack() as scope:
            gr = sb_in(scope, "gla_gate", [P, 4, T])
            linear(4, 8, from_h, ["act"] * 4, act_to(lambda m: gr[:, m], ACT.Silu))
            norm(lambda t: Y[:, t], 4, 4, P, lambda t: V("gla_norm_w", t), lambda t: Y[:, t], gate=lambda t: gr[:, t])

        merged = sb("merged", [P, DT, T])

        def from_y(u, k, h):
            return Y[:, k, h * HALF:(h + 1) * HALF]

        def merge(b):
            with ExitStack() as scope:
                g = sb_in(scope, f"gates{b}", [P, DT, T])

                def sig(e, link, m, u, src, i):
                    return nc.scalar.activation(g[:, m], src, ACT.Sigmoid,
                                                bias=V("gate_b", 0, 24)[:, bass.ds(m + 8 * b, 1)])
                linear(8, 8, from_h, ["act"] * 4, sig)

                def emit(e, link, m, u, src, i):
                    if b == 0:
                        return nc.vector.tensor_tensor(merged[:, m], src, g[:, m], ALU.mult)
                    link(nc.vector.tensor_tensor(g[:, m], src, g[:, m], ALU.mult))
                    return nc.vector.tensor_tensor(merged[:, m], merged[:, m], g[:, m], ALU.add)
                linear(8, 4, from_y, ["dve"] * 8, emit)
        merge(0)

        def conv_silu(raw, n, w, b, out, func):
            b_dve = dve_out.n
            with nc.Block() as block:
                @block.vector
                def _(dve):
                    link = Link(dve, dve_own)
                    for t in range(n):
                        link(nc.vector.tensor_scalar(out[:, t], raw[:, t, 3:3 + T], w(3, t), b(t), ALU.mult, ALU.add))
                        for tap in range(3):
                            ins = nc.vector.scalar_tensor_tensor(out[:, t], raw[:, t, tap:tap + T], w(tap, t),
                                                                 out[:, t], ALU.mult, ALU.add)
                            if tap < 2 or func is None:
                                link(ins)
                            else:
                                ins.then_inc(dve_out.sem, 1)
                    link.close()

                @block.scalar
                def _(act):
                    if func is not None:
                        for t in range(n):
                            act.wait_ge(dve_out.sem, b_dve + t + 1)
                            nc.scalar.activation(out[:, t], out[:, t], func)
            if func is not None:
                dve_out.n += n

        def zero_front(raw, n):
            with nc.Block() as block:
                @block.vector
                def _(dve):
                    nc.vector.memset(raw[:, :, 0:3], 0.0)

        with ExitStack() as scope:
            qk = sb_in(scope, "ml_qk", [P, 4, T])
            v = sb_in(scope, "ml_v", [P, CH, 4 * P])
            Mb = sb_in(scope, "ml_max", [P, HEADS, T])
            eb = sb_in(scope, "ml_floor", [P, HEADS, T])
            Gc = sb_in(scope, "ml_gain", [P, CH, HEADS])
            with ExitStack() as s2:
                raw = sb_in(s2, "ml_raw", [P, 4, 3 + T])
                zero_front(raw, 4)
                linear(4, 8, from_h, ["act", "dve", "act", "dve"], copy_to(lambda m: raw[:, m, 3:3 + T]))
                conv_silu(raw, 4, lambda tap, t: V("conv_w", 4 * tap + t), lambda t: V("conv_b", t), qk, ACT.Silu)
            token_major(CH, 4 * P, DT, lambda k, c: H[:, k, c * P:(c + 1) * P], lambda c, op, src: op(v[:, c], src))
            with ExitStack() as s2:
                t0 = sb_in(s2, "ml_t0", [HEADS, T])
                t1 = sb_in(s2, "ml_t1", [HEADS, T])
                one = sb_in(s2, "ml_one", [HEADS, T])
                li = sb_in(s2, "ml_i", [HEADS, T])
                lf = sb_in(s2, "ml_f", [HEADS, T])
                G = sb_in(s2, "ml_G", [HEADS, T])
                M = sb_in(s2, "ml_M", [HEADS, T])
                m_ = sb_in(s2, "ml_m", [HEADS, T])
                base, b_act, b_dve, b_own = pe_done.n, act_out.n, dve_out.n, act_own.n
                with nc.Block() as block:
                    @block.vector
                    def _(dve):
                        link = Link(dve, dve_own)
                        link(nc.vector.memset(one[:], 1.0))
                        link(nc.vector.tensor_scalar(li[:], small[:, 0], V("i_b")[0:HEADS], None, ALU.add))
                        link(nc.vector.tensor_scalar(lf[:], small[:, 1], V("f_b")[0:HEADS], None, ALU.add))
                        nc.vector.scalar_tensor_tensor(t0[:], lf[:], -1.0, lf[:], ALU.mult, ALU.max).then_inc(dve_out.sem, 1)
                        dve.wait_ge(act_out.sem, b_act + 1)
                        link(nc.vector.scalar_tensor_tensor(lf[:], lf[:], 0.0, t1[:], ALU.min, ALU.subtract))
                        link(nc.vector.tensor_tensor_scan(t0[:], one[:], lf[:], 0.0, ALU.mult, ALU.add))
                        link(nc.vector.tensor_tensor(G[:], li[:], t0[:], ALU.subtract))
                        link(nc.vector.tensor_tensor_scan(M[:], G[:], G[:], 0.0, ALU.max, ALU.max))
                        nc.vector.tensor_tensor(m_[:], t0[:], M[:], ALU.add).then_inc(dve_out.sem, 1)
                        dve.wait_ge(pe_done.sem, base + 1)
                        nc.vector.tensor_copy(Gc[:].rearrange("p c h -> p (c h)"), ps[:, 0, 0:CH * HEADS]
                                              ).then_inc(dve_free.sem, 1)
                        for h in range(HEADS):
                            dve.wait_ge(pe_done.sem, base + 2 + 2 * h)
                            nc.vector.tensor_copy(Mb[:, h], pair[(2 * h + 1) % 4]).then_inc(dve_free.sem, 1)
                        link.close()

                    @block.scalar
                    def _(act):
                        act.wait_ge(dve_out.sem, b_dve + 1)
                        nc.scalar.activation(t1[:], t0[:], ACT.Exp, scale=-1.0).then_inc(act_own.sem, 1)
                        act.wait_ge(act_own.sem, b_own + 1)
                        nc.scalar.activation(t1[:], t1[:], ACT.Ln, bias=1.0).then_inc(act_out.sem, 1)
                        for h in range(HEADS):
                            act.wait_ge(pe_done.sem, base + 3 + 2 * h)
                            nc.scalar.activation(eb[:, h], pair[(2 * h + 2) % 4], ACT.Exp, scale=-1.0
                                                 ).then_inc(act_free.sem, 1)

                    @block.tensor
                    def _(pe):
                        pe.wait_ge(dve_out.sem, b_dve + 2)
                        for c in range(CH):
                            mm = nc.tensor.transpose(ps[:, 0, c * HEADS:(c + 1) * HEADS], G[:, c * P:(c + 1) * P],
                                                     ident[0:HEADS, 0:HEADS])
                        mm.then_inc(pe_done.sem, 1)
                        for h in range(HEADS):
                            pick = C("sel", h * P, (h + 1) * P)[0:HEADS]
                            for j, src in enumerate((M, m_)):
                                job = 2 * h + 1 + j
                                if job >= 4:
                                    if job == 4:
                                        pe.wait_ge(dve_free.sem, dve_free.n + 1)
                                    elif (job - 4) % 2:
                                        pe.wait_ge(dve_free.sem, dve_free.n + 1 + (job - 4 + 1) // 2)
                                    else:
                                        pe.wait_ge(act_free.sem, act_free.n + (job - 4) // 2)
                                for half in range(2):
                                    cols = slice(half * HALF, (half + 1) * HALF)
                                    mm = nc.tensor.matmul(pair[job % 4][:, cols], pick, src[:, cols], start=True,
                                                          stop=True)
                                mm.then_inc(pe_done.sem, 1)
                pe_done.n += 1 + 2 * HEADS
                act_own.n += 1
                act_out.n += 1
                dve_out.n += 2
                dve_free.n += 1 + HEADS
                act_free.n += HEADS

            with ExitStack() as s2:
                arg = sb_in(s2, "ml_arg", [P, 2, P])
                wt = sb_in(s2, "ml_wt", [P, 3, HALF])
                pr = sb_in(s2, "ml_pr", [P, 3, HALF])
                den = sb_in(s2, "ml_den", [P, 2, HALF])
                steps = [(h, t, s) for h in range(HEADS) for t in range(2) for s in range(4 * t + 4)]
                groups = [(h, t) for h in range(HEADS) for t in range(2)]
                ends = [n for n, (h, t, s) in enumerate(steps) if s == 4 * t + 3]
                b_s, b_o, b_p, b_do, b_act, b_out = pe_s.n, pe_o.n, act_p.n, dve_o.n, act_out.n, dve_out.n
                diag_steps = [n for n, (h, t, s) in enumerate(steps) if s >= 4 * t]
                span = lambda t, s: (max(HALF * t, P * s), HALF * (t + 1))

                arg_ready = sem("ml_arg_ready")

                def scaled_keys(h, s):
                    return qk[64 * (h % 2):64 * (h % 2) + 64, 2 + h // 2, s * P:(s + 1) * P]

                with nc.Block() as block:
                    @block.tensor
                    def _(pe):
                        def weigh(n):
                            h, t, s = steps[n]
                            lo, hi = span(t, s)
                            g = groups.index((h, t))
                            pe.wait_ge(dve_out.sem, b_out + n + 1)
                            if s == 0 and g >= 2:
                                pe.wait_ge(dve_o.sem, b_do + g - 1)
                            o = slice(lo - HALF * t, HALF)
                            nc.tensor.matmul(ps[:, 4 + 2 * (g % 2), o], v[:, s, h * P:(h + 1) * P],
                                             pr[:, n % 3, 0:hi - lo], start=(s == 0), stop=(s == 4 * t + 3))
                            nc.tensor.matmul(ps[:, 5 + 2 * (g % 2), o], ones, pr[:, n % 3, 0:hi - lo],
                                             start=(s == 0), stop=(s == 4 * t + 3)).then_inc(pe_o.sem, 1)
                        for n, (h, t, s) in enumerate(steps):
                            lo, hi = span(t, s)
                            if n >= 3:
                                pe.wait_ge(dve_out.sem, b_out + n - 2)
                            nc.tensor.matmul(ps[:, n % 3, 0:hi - lo], scaled_keys(h, s),
                                             qk[64 * (h % 2):64 * (h % 2) + 64, h // 2, lo:hi],
                                             start=True, stop=True).then_inc(pe_s.sem, 1)
                            if n >= 2:
                                weigh(n - 2)
                        weigh(len(steps) - 2)
                        weigh(len(steps) - 1)

                    @block.scalar
                    def _(act):
                        for n, (h, t, s) in enumerate(steps):
                            lo, hi = span(t, s)
                            if n >= 3:
                                act.wait_ge(dve_out.sem, b_out + n - 2)
                            if s >= 4 * t:
                                d = diag_steps.index(n)
                                act.wait_ge(arg_ready.sem, d + 1)
                                ins = nc.scalar.activation(wt[:, n % 3, 0:P], arg[:, d % 2], ACT.Exp,
                                                           bias=Gc[:, s, h:h + 1], scale=-1.0)
                                if hi - lo > P:
                                    ins = nc.scalar.activation(wt[:, n % 3, P:hi - lo], Mb[:, h, lo + P:hi], ACT.Exp,
                                                               bias=Gc[:, s, h:h + 1], scale=-1.0)
                            else:
                                ins = nc.scalar.activation(wt[:, n % 3, 0:hi - lo], Mb[:, h, lo:hi], ACT.Exp,
                                                           bias=Gc[:, s, h:h + 1], scale=-1.0)
                            ins.then_inc(act_p.sem, 1)

                    @block.vector
                    def _(dve):
                        link = Link(dve, dve_own)

                        def exponent(d):
                            if d >= len(diag_steps):
                                return
                            h, t, s = steps[diag_steps[d]]
                            if d >= 2:
                                dve.wait_ge(act_p.sem, b_p + diag_steps[d - 2] + 1)
                            nc.vector.tensor_tensor(arg[:, d % 2], Mb[:, h, s * P:(s + 1) * P], C("mask_kq"),
                                                    ALU.subtract).then_inc(arg_ready.sem, 1)
                        exponent(0)
                        exponent(1)
                        d = 2
                        for n, (h, t, s) in enumerate(steps):
                            lo, hi = span(t, s)
                            dve.wait_ge(pe_s.sem, b_s + n + 1)
                            dve.wait_ge(act_p.sem, b_p + n + 1)
                            if n >= 3:
                                dve.wait_ge(pe_o.sem, b_o + n - 2)
                            nc.vector.scalar_tensor_tensor(pr[:, n % 3, 0:hi - lo], ps[:, n % 3, 0:hi - lo],
                                                           DK ** -0.5, wt[:, n % 3, 0:hi - lo], ALU.mult,
                                                           ALU.mult).then_inc(dve_out.sem, 1)
                            if n in diag_steps:
                                exponent(d)
                                d += 1
                            if n in ends:
                                g = groups.index((h, t))
                                dve.wait_ge(pe_o.sem, b_o + n + 1)
                                link(nc.vector.scalar_tensor_tensor(den[:, 0], ps[:, 5 + 2 * (g % 2)], -1.0,
                                                                    eb[:, h, HALF * t:HALF * (t + 1)], ALU.mult,
                                                                    ALU.max))
                                link(nc.vector.tensor_tensor(den[:, 0], ps[:, 5 + 2 * (g % 2)], den[:, 0], ALU.max))
                                link(nc.vector.reciprocal(den[:, 1], den[:, 0]))
                                ins = nc.vector.tensor_tensor(Y[:, h, HALF * t:HALF * (t + 1)],
                                                              ps[:, 4 + 2 * (g % 2)], den[:, 1], ALU.mult)
                                ins.then_inc(dve_o.sem, 1)
                                dve.wait_ge(dve_o.sem, b_do + g + 1)
                        link.close()
                pe_s.n += len(steps)
                pe_o.n += len(steps)
                act_p.n += len(steps)
                dve_out.n += len(steps)
                dve_o.n += len(groups)
        with ExitStack() as scope:
            og = sb_in(scope, "ml_gate", [P, 4, T])

            def emit(e, link, m, u, src, i):
                link(nc.scalar.activation(og[:, m], src, ACT.Sigmoid))
                return nc.scalar.activation(og[:, m], og[:, m], ACT.Copy)
            linear(4, 8, from_h, ["act"] * 4, emit)
            with nc.Block() as block:
                @block.vector
                def _(dve):
                    for t in range(4):
                        nc.vector.tensor_tensor(Y[:, t], Y[:, t], og[:, t], ALU.mult)
        merge(1)

        with ExitStack() as scope:
            u_ = sb_in(scope, "s5_u", [P, 4, T])
            bT = sb_in(scope, "s5_bT", [P, 2, 4, P])
            cT = sb_in(scope, "s5_cT", [P, 2, 16, 32])
            mag = sb_in(scope, "s5_mag", [P, 16])
            coarse = sb_in(scope, "s5_coarse", [P, 16, 32])
            fine = sb_in(scope, "s5_fine", [P, 16, 32])
            linear(4, 8, from_h, ["act", "dve", "act", "dve"], copy_to(lambda m: u_[:, m]))
            with ExitStack() as s2:
                b_raw = sb_in(s2, "s5_b", [P, 2, 16, 32])
                bb = sb_in(s2, "s5_bbar", [P, 2, 16, 32])
                tmp = sb_in(s2, "s5_tmp", [P, 16, 32])
                w = sb_in(s2, "s5_w", [P, 16, 16])
                W = lambda j: w[:, j]
                with nc.Block() as block:
                    @block.sync
                    def _(sp):
                        sp.dma_start(b_raw[:], a["s5_b"]).then_inc(loaded.sem, 16)
                        sp.dma_start(cT[:], a["s5_c"]).then_inc(loaded.sem, 16)
                        loaded.n += 32
                        sp.wait_ge(loaded.sem, loaded.n)
                base, b_act, b_dve = pe_done.n, act_out.n, dve_out.n
                with nc.Block() as block:
                    @block.scalar
                    def _(act):
                        nc.scalar.activation(W(0), V("log_step", 0, 16), ACT.Exp).then_inc(act_out.sem, 1)
                        act.wait_ge(dve_out.sem, b_dve + 1)
                        nc.scalar.activation(mag[:], W(2), ACT.Exp).then_inc(act_out.sem, 1)
                        act.wait_ge(dve_out.sem, b_dve + 2)
                        nc.scalar.activation(W(6), W(5), ACT.Sin, scale=6.283185)
                        nc.scalar.activation(W(7), W(5), ACT.Sin, scale=3.1415925).then_inc(act_out.sem, 1)

                    @block.vector
                    def _(dve):
                        link = Link(dve, dve_own)
                        tt = nc.vector.tensor_tensor
                        ts = nc.vector.tensor_scalar
                        link(ts(W(1), V("lam_re", 0, 16), -1e-4, None, ALU.min))
                        dve.wait_ge(act_out.sem, b_act + 1)
                        tt(W(2), W(1), W(0), ALU.mult).then_inc(dve_out.sem, 1)
                        link(tt(W(3), V("lam_im", 0, 16), W(0), ALU.mult))
                        link(ts(W(3), W(3), 1.0 / TWO_PI, None, ALU.mult))
                        link(ts(W(4), W(3), MAGIC, MAGIC, ALU.add, ALU.subtract))
                        tt(W(5), W(3), W(4), ALU.subtract).then_inc(dve_out.sem, 1)
                        dve.wait_ge(act_out.sem, b_act + 3)
                        link(tt(W(7), W(7), W(7), ALU.mult))
                        link(ts(W(7), W(7), -2.0, 1.0, ALU.mult, ALU.add))
                        link(tt(W(8), mag[:], W(7), ALU.mult))
                        link(tt(W(9), mag[:], W(6), ALU.mult))
                        link(tt(W(10), W(1), W(1), ALU.mult))
                        link(tt(W(11), V("lam_im", 0, 16), V("lam_im", 0, 16), ALU.mult))
                        link(tt(W(10), W(10), W(11), ALU.add))
                        link(nc.vector.reciprocal(W(10), W(10)))
                        link(ts(W(8), W(8), 1.0, None, ALU.subtract))
                        link(tt(W(11), W(8), W(1), ALU.mult))
                        link(tt(W(12), W(9), V("lam_im", 0, 16), ALU.mult))
                        link(tt(W(11), W(11), W(12), ALU.add))
                        link(tt(W(13), W(11), W(10), ALU.mult))
                        link(tt(W(11), W(9), W(1), ALU.mult))
                        link(tt(W(12), W(8), V("lam_im", 0, 16), ALU.mult))
                        link(tt(W(11), W(11), W(12), ALU.subtract))
                        link(tt(W(14), W(11), W(10), ALU.mult))
                        zr = W(13).unsqueeze(2).broadcast_to([P, 16, 32])
                        zi = W(14).unsqueeze(2).broadcast_to([P, 16, 32])
                        link(tt(bb[:, 0], b_raw[:, 0], zr, ALU.mult))
                        link(tt(tmp[:], b_raw[:, 1], zi, ALU.mult))
                        link(tt(bb[:, 0], bb[:, 0], tmp[:], ALU.subtract))
                        link(tt(bb[:, 1], b_raw[:, 1], zr, ALU.mult))
                        link(tt(tmp[:], b_raw[:, 0], zi, ALU.mult))
                        tt(bb[:, 1], bb[:, 1], tmp[:], ALU.add).then_inc(dve_out.sem, 1)
                        ramp = C("ramp").unsqueeze(1).broadcast_to([P, 16, 32])
                        link(tt(fine[:], W(5).unsqueeze(2).broadcast_to([P, 16, 32]), ramp, ALU.mult))
                        link(ts(W(11), W(5), 32.0, None, ALU.mult))
                        link(ts(W(12), W(11), MAGIC, MAGIC, ALU.add, ALU.subtract))
                        link(tt(W(11), W(11), W(12), ALU.subtract))
                        link(tt(coarse[:], W(11).unsqueeze(2).broadcast_to([P, 16, 32]), ramp, ALU.mult))
                        link(ts(tmp[:], coarse[:], MAGIC, MAGIC, ALU.add, ALU.subtract))
                        link(tt(coarse[:], coarse[:], tmp[:], ALU.subtract))
                        link(ts(cT[:, 1], cT[:, 1], -1.0, None, ALU.mult))
                        dve.wait_ge(pe_done.sem, base + 1)
                        nc.vector.tensor_copy(bT[:].rearrange("p r q m -> p (r q m)"), pair[0]).then_inc(dve_out.sem, 1)
                        link.close()

                    @block.tensor
                    def _(pe):
                        pe.wait_ge(dve_out.sem, b_dve + 3)
                        for r in range(2):
                            for g in range(4):
                                mm = nc.tensor.transpose(pair[0][:, (r * 4 + g) * P:(r * 4 + g + 1) * P],
                                                         bb[:, r, 4 * g:4 * g + 4].rearrange("p t c -> p (t c)"), ident)
                        mm.then_inc(pe_done.sem, 1)
                pe_done.n += 1
                act_out.n += 3
                dve_out.n += 4
            with ExitStack() as s2:
                ph = sb_in(s2, "s5_phase", [P, 2, T])
                sn = sb_in(s2, "s5_sin", [P, 2, T])
                cs = sb_in(s2, "s5_cos", [P, 2, T])
                br = sb_in(s2, "s5_br", [P, 2, T])
                bi = sb_in(s2, "s5_bi", [P, 2, T])
                xr = sb_in(s2, "s5_xr", [P, 2, T])
                xi = sb_in(s2, "s5_xi", [P, 2, T])
                m1 = sb_in(s2, "s5_m1", [P, T])
                g1 = sb_in(s2, "s5_g1", [P, T])
                b_pe, b_act, b_dve, b_pool = pe_done.n, act_out.n, dve_out.n, pool_out.n
                b_free, b_o, b_do = dve_free.n, pe_o.n, dve_o.n
                with nc.Block() as block:
                    @block.tensor
                    def _(pe):
                        def bu(t):
                            r = slice(32 * (t % 4), 32 * (t % 4) + 32)
                            if t >= 1:
                                pe.wait_ge(dve_free.sem, b_free + t)
                            for part in range(2):
                                for h in range(2):
                                    mm = nc.tensor.matmul(pair[part][:, h * HALF:(h + 1) * HALF], bT[r, part, t // 4],
                                                          u_[r, t // 4, h * HALF:(h + 1) * HALF], start=True, stop=True,
                                                          tile_position=(32 * (t % 4), 0))
                            mm.then_inc(pe_done.sem, 1)

                        def cx(t):
                            pe.wait_ge(dve_out.sem, b_dve + 2 * t + 2)
                            pe.wait_ge(pool_out.sem, b_pool + 2 * t + 2)
                            q_ = t // 4
                            if t % 4 == 0 and q_ >= 2:
                                pe.wait_ge(dve_o.sem, b_do + q_ - 1)
                            for h in range(2):
                                o = pair[2 + q_ % 2][32 * (t % 4):32 * (t % 4) + 32, h * HALF:(h + 1) * HALF]
                                nc.tensor.matmul(o, cT[:, 0, t], xr[:, t % 2, h * HALF:(h + 1) * HALF], start=True,
                                                 stop=False, tile_position=(0, 32 * (t % 4)))
                                mm = nc.tensor.matmul(o, cT[:, 1, t], xi[:, t % 2, h * HALF:(h + 1) * HALF],
                                                      start=False, stop=True, tile_position=(0, 32 * (t % 4)))
                            mm.then_inc(pe_o.sem, 1)
                        bu(0)
                        for t in range(16):
                            if t < 15:
                                bu(t + 1)
                            cx(t)

                    @block.scalar
                    def _(act):
                        for t in range(16):
                            act.wait_ge(pool_out.sem, b_pool + 2 * t + 1)
                            nc.scalar.activation(sn[:, t % 2], ph[:, t % 2], ACT.Sin, scale=6.283185)
                            nc.scalar.activation(cs[:, t % 2], ph[:, t % 2], ACT.Sin, scale=3.1415925
                                                 ).then_inc(act_own.sem, 1)
                            act.wait_ge(act_own.sem, act_own.n + 2 * t + 1)
                            nc.scalar.activation(cs[:, t % 2], cs[:, t % 2], ACT.Square).then_inc(act_own.sem, 1)
                            act.wait_ge(act_own.sem, act_own.n + 2 * t + 2)
                            nc.scalar.activation(cs[:, t % 2], cs[:, t % 2], ACT.Copy, bias=1.0, scale=-2.0
                                                 ).then_inc(act_out.sem, 1)
                        act_own.n += 32

                    @block.gpsimd
                    def _(pool):
                        link = Link(pool, pool_own)
                        tt = nc.gpsimd.tensor_tensor

                        def phase(t):
                            if t >= 2:
                                pool.wait_ge(dve_out.sem, b_dve + 2 * (t - 2) + 2)
                            p3 = ph[:, t % 2].rearrange("p (a b) -> p a b", b=32)
                            link(tt(p3, coarse[:, t].unsqueeze(2).broadcast_to([P, 32, 32]),
                                    fine[:, t].unsqueeze(1).broadcast_to([P, 32, 32]), ALU.add))
                            link(nc.gpsimd.tensor_scalar(g1[:], ph[:, t % 2], MAGIC, MAGIC, ALU.add,
                                                         ALU.subtract))
                            tt(ph[:, t % 2], ph[:, t % 2], g1[:], ALU.subtract).then_inc(pool_out.sem, 1)

                        phase(0)
                        for t in range(16):
                            pool.wait_ge(dve_out.sem, b_dve + 2 * t + 1)
                            pool.wait_ge(act_out.sem, b_act + t + 1)
                            if t >= 2:
                                pool.wait_ge(pe_o.sem, b_o + t - 1)
                            link(tt(g1[:], br[:, t % 2], sn[:, t % 2], ALU.mult))
                            link(tt(xi[:, t % 2], bi[:, t % 2], cs[:, t % 2], ALU.mult))
                            tt(xi[:, t % 2], xi[:, t % 2], g1[:], ALU.add).then_inc(pool_out.sem, 1)
                            pool.wait_ge(pool_out.sem, b_pool + 2 * t + 2)
                            if t < 15:
                                phase(t + 1)
                        link.close()

                    @block.vector
                    def _(dve):
                        link = Link(dve, dve_own)
                        tt = nc.vector.tensor_tensor
                        for t in range(16):
                            b = t % 2
                            dve.wait_ge(pe_done.sem, b_pe + t + 1)
                            dve.wait_ge(act_out.sem, b_act + t + 1)
                            if t >= 2:
                                dve.wait_ge(pool_out.sem, b_pool + 2 * (t - 2) + 2)
                            link(tt(m1[:], pair[0], cs[:, b], ALU.mult))
                            link(tt(br[:, b], pair[1], sn[:, b], ALU.mult))
                            link(tt(br[:, b], br[:, b], m1[:], ALU.add))
                            link(tt(m1[:], pair[1], cs[:, b], ALU.mult))
                            tt(bi[:, b], pair[0], sn[:, b], ALU.mult).then_inc(dve_free.sem, 1)
                            dve.wait_ge(dve_free.sem, b_free + t + 1)
                            link(tt(bi[:, b], m1[:], bi[:, b], ALU.subtract))
                            decay = mag[:, t:t + 1].broadcast_to([P, T])
                            link(nc.vector.tensor_tensor_scan(br[:, b], decay, br[:, b], 0.0, ALU.mult, ALU.add))
                            nc.vector.tensor_tensor_scan(bi[:, b], decay, bi[:, b], 0.0, ALU.mult, ALU.add
                                                         ).then_inc(dve_out.sem, 1)
                            dve.wait_ge(dve_out.sem, b_dve + 2 * t + 1)
                            if t >= 2:
                                dve.wait_ge(pe_o.sem, b_o + t - 1)
                            link(tt(m1[:], br[:, b], cs[:, b], ALU.mult))
                            link(tt(xr[:, b], bi[:, b], sn[:, b], ALU.mult))
                            tt(xr[:, b], m1[:], xr[:, b], ALU.subtract).then_inc(dve_out.sem, 1)
                            dve.wait_ge(dve_out.sem, b_dve + 2 * t + 2)
                            if t % 4 == 3:
                                q_ = t // 4
                                dve.wait_ge(pe_o.sem, b_o + t + 1)
                                nc.vector.scalar_tensor_tensor(Y[:, q_], u_[:, q_], V("s5_d", q_), pair[2 + q_ % 2],
                                                               ALU.mult, ALU.add).then_inc(dve_o.sem, 1)
                        link.close()
                pe_done.n += 16
                pe_o.n += 16
                act_out.n += 16
                pool_out.n += 32
                dve_out.n += 32
                dve_free.n += 16
                dve_o.n += 4
            with nc.Block() as block:
                @block.scalar
                def _(act):
                    for t in range(4):
                        nc.scalar.activation(Y[:, t], Y[:, t], ACT.Gelu_apprx_tanh)
            linear(4, 4, from_y, ["act"] * 4, act_to(lambda m: u_[:, m], ACT.Sigmoid, bias=lambda m: V("glu_b", m)))
            with nc.Block() as block:
                @block.vector
                def _(dve):
                    for t in range(4):
                        nc.vector.tensor_tensor(Y[:, t], Y[:, t], u_[:, t], ALU.mult)
        merge(2)

        def from_merged(u, k, h):
            return merged[:, k, h * HALF:(h + 1) * HALF]
        linear(8, 8, from_merged, ["act", "dve", "act", "dve"], copy_to(lambda m: H[:, m]))
        x1 = merged
        with ExitStack() as scope:
            x0 = sb_in(scope, "x0_again", [P, DT, T])
            load(x0[:], a["x"])
            norm(lambda t: H[:, t], DT, 1, D, lambda t: fold[:, 8 + t:9 + t], lambda t: x1[:, t],
                 residual=lambda t: x0[:, t])

        norm(lambda t: x1[:, t], DT, 1, D, lambda t: fold[:, 16 + t:17 + t], lambda t: H[:, t],
             bias=lambda t: mod[:, 24 + t:25 + t])
        with ExitStack() as scope:
            hid = sb_in(scope, "ffn_hidden", [P, FT, T])
            b_free = act_free.n

            def emit(e, link, m, u, src, i):
                tile = i * 2 + u // 2
                if e == "act":
                    link(nc.scalar.activation(hid[:, tile], src, ACT.Silu))
                    return nc.scalar.activation(act0[:, 4:5], act0[:, 4:5], ACT.Copy)
                link.eng.wait_ge(act_free.sem, i * 2 + (b_free + u // 2 + 1))
                return nc.vector.tensor_tensor(hid[:, tile], hid[:, tile], src, ALU.mult)
            linear(2 * FT, 8, from_h, ["act", "dve", "act", "dve"], emit, own={"act": 2})
            linear(DT, FT, lambda u, k, h: hid[:, k, h * HALF:(h + 1) * HALF], ["act", "dve", "act", "dve"],
                   copy_to(lambda m: H[:, m]), ktp=24)
        norm(lambda t: H[:, t], DT, 1, D, lambda t: fold[:, 24 + t:25 + t], lambda t: H[:, t],
             residual=lambda t: x1[:, t])

        Z = merged

        def heads_in_halves(dest):
            def emit(e, link, m, u, src, i):
                for j in range(2):
                    out = dest(2 * m + j)
                    if e == "act":
                        ins = nc.scalar.activation(out, src[64 * j:64 * j + 64], ACT.Copy)
                    else:
                        ins = nc.vector.tensor_copy(out, src[64 * j:64 * j + 64])
                return ins
            return emit

        def attention(iters, U, dq, keys_n, scale, q_of, k_of, v_of, out_of, sfx, project=None):
            causal = project is not None
            seq = []
            if causal:
                seq = [("P", 0), ("P", 1)]
            seq += [("A", 0), ("R", 0), ("A", 1)]
            for u in range(U):
                seq.append(("S", u))
                if u + 1 < U:
                    seq.append(("R", u + 1))
                if u + 2 < U:
                    seq += ([("P", u + 2)] if causal else []) + [("A", u + 2)]
            jobs = []
            for kind, u in seq:
                if kind == "P":
                    jobs += [("Q", u, 0), ("K", u, 0), ("V", u, 0)]
                if kind == "A":
                    jobs += [("A", u, b) for b in range(CH if causal else 2)]
                if kind == "R":
                    jobs += [("R", u, 0)]
            readers = {"Q": ("act", "dve"), "K": ("act",), "V": ("act",), "A": ("dve",), "R": ("dve",)}
            after = {"act": [], "dve": []}
            for kind, u, b in jobs:
                for e in after:
                    after[e].append((after[e][-1] if after[e] else 0) + (e in readers[kind]))
            J = len(jobs)
            assert J % 2 == 0 or iters == 1
            at = {job: n for n, job in enumerate(jobs)}
            if causal:
                steps = [(u, t, s) for u in range(U) for t in range(2) for s in range(4 * t + 4)]
                last = lambda t: 4 * t + 3
            else:
                steps = [(u, t, s) for u in range(U) for t in range(2) for s in range(keys_n // P)]
                last = lambda t: keys_n // P - 1
            step_at = {st: n for n, st in enumerate(steps)}
            span = lambda t, s: (max(HALF * t, P * s) if causal else HALF * t, HALF * (t + 1))
            base, b_s, b_o, b_p, b_do = pe_done.n, pe_s.n, pe_o.n, act_p.n, dve_o.n
            b_e = {"act": act_free.n, "dve": dve_free.n}
            s0 = stream["slot"]

            def val(i, per, value):
                if i is None:
                    return value
                assert value >= 0
                return i * per + value

            with ExitStack() as scope:
                mx = sb_in(scope, "att_max" + sfx, [P, 2, CH])
                pr = sb_in(scope, "att_p" + sfx, [P, 4, HALF])
                rec = sb_in(scope, "att_rec" + sfx, [P, HALF])
                t_a = sb_in(scope, "att_ta" + sfx, [P, T]) if causal else None
                t_b = sb_in(scope, "att_tb" + sfx, [P, T]) if causal else None

                def looped(eng, body):
                    if iters == 1:
                        body(None)
                    else:
                        with eng.Fori(0, iters, 1) as i:
                            body(i)

                with nc.Block() as block:
                    if causal:
                        @block.sync
                        def _(sp):
                            looped(sp, lambda i: refill(sp, i, s0, U, [at[("V", u, 0)] + 1 for u in range(U)], base, J))

                    @block.tensor
                    def _(pe):
                        def body(i):
                            reached = {"act": -1, "dve": -1}

                            def reads_of(e, value):
                                if value > reached[e]:
                                    reached[e] = value
                                    pe.wait_ge(free[e].sem, val(i, after[e][-1], value))

                            def pair_of(job):
                                j = at[job]
                                if j >= 2 or i is not None:
                                    before = (j - 2) % J
                                    for e in readers[jobs[before][0]]:
                                        per = after[e][-1]
                                        value = b_e[e] + after[e][before] - (per if j < 2 else 0)
                                        reads_of(e, value)
                                return pair[j % 2]

                            def evacuated(e, job):
                                reads_of(e, b_e[e] + after[e][at[job]])

                            def weigh(n):
                                u, t, s = steps[n]
                                lo, hi = span(t, s)
                                g = 2 * u + t
                                pe.wait_ge(act_p.sem, val(i, len(steps), b_p + n + 1))
                                if s == 0 and (g >= 2 or i is not None):
                                    pe.wait_ge(dve_o.sem, val(i, 2 * U, b_do + g - 1))
                                nc.tensor.matmul(ps[:, 6 + t, lo - HALF * t:HALF], v_of(u, s), pr[:, n % 4, 0:hi - lo],
                                                 start=(s == 0), stop=(s == last(t))).then_inc(pe_o.sem, 1)

                            for kind, u in seq:
                                if kind == "P":
                                    project(pe, i, u, pair_of, s0)
                                if kind == "A":
                                    if causal:
                                        evacuated("act", ("V", u, 0))
                                        evacuated("dve", ("Q", u, 0))
                                    for b in range(CH if causal else 2):
                                        o = pair_of(("A", u, b))
                                        if causal:
                                            n_keys = (b + 1) * P
                                            for lo in range(0, n_keys, HALF):
                                                hi = min(lo + HALF, n_keys)
                                                nc.tensor.matmul(o[:, lo:hi], q_of(u)[0:dq, b * P:(b + 1) * P],
                                                                 k_of(u)[0:dq, lo:hi], start=True, stop=(hi != n_keys))
                                            mm = nc.tensor.matmul(o[:, b * P:n_keys], ident, C("mask_qk"), start=False,
                                                                  stop=True)
                                        else:
                                            for j in range(4):
                                                mm = nc.tensor.matmul(
                                                    o[:, j * MEM:(j + 1) * MEM],
                                                    q_of(u)[0:dq, (4 * b + j) * P:(4 * b + j + 1) * P],
                                                    k_of(u)[0:dq], start=True, stop=True)
                                        mm.then_inc(pe_done.sem, 1)
                                if kind == "R":
                                    evacuated("dve", ("A", u, (CH if causal else 2) - 1))
                                    o = pair_of(("R", u, 0))
                                    for c in range(CH):
                                        mm = nc.tensor.matmul(o[dq:dq + 1, c * P:(c + 1) * P], mx[:, u % 2, c:c + 1],
                                                              ident, start=True, stop=True)
                                    mm.then_inc(pe_done.sem, 1)
                                if kind == "S":
                                    evacuated("dve", ("R", u, 0))
                                    mine = [n for n, st in enumerate(steps) if st[0] == u]
                                    for n in mine:
                                        _, t, s = steps[n]
                                        lo, hi = span(t, s)
                                        if n >= 2 or i is not None:
                                            pe.wait_ge(act_p.sem, val(i, len(steps), b_p + n - 1))
                                        diag = causal and s >= 4 * t
                                        mm = nc.tensor.matmul(ps[:, 4 + n % 2, 0:hi - lo],
                                                              k_of(u)[0:dq + 1, s * P:(s + 1) * P],
                                                              q_of(u)[0:dq + 1, lo:hi], start=True, stop=not diag)
                                        if diag:
                                            mm = nc.tensor.matmul(ps[:, 4 + n % 2, 0:P], ident, C("mask_kq"),
                                                                  start=False, stop=True)
                                        mm.then_inc(pe_s.sem, 1)
                                        if n > mine[0]:
                                            weigh(n - 1)
                                    weigh(mine[-1])
                        looped(pe, body)

                    @block.scalar
                    def _(act):
                        def body(i):
                            for kind, u in seq:
                                if kind == "P":
                                    for part in ("Q", "K", "V"):
                                        j = at[(part, u, 0)]
                                        act.wait_ge(pe_done.sem, val(i, J, base + j + 1))
                                        project.take(part, u, pair[j % 2]).then_inc(act_free.sem, 1)
                                if kind == "S":
                                    for n, (u2, t, s) in enumerate(steps):
                                        if u2 != u:
                                            continue
                                        lo, hi = span(t, s)
                                        act.wait_ge(pe_s.sem, val(i, len(steps), b_s + n + 1))
                                        if n >= 4 or i is not None:
                                            act.wait_ge(pe_o.sem, val(i, len(steps), b_o + n - 3))
                                        nc.scalar.activation(pr[:, n % 4, 0:hi - lo], ps[:, 4 + n % 2, 0:hi - lo],
                                                             ACT.Exp, scale=scale).then_inc(act_p.sem, 1)
                        looped(act, body)

                    dve_links = U * ((2 if causal else 0) + 2)

                    @block.vector
                    def _(dve):
                        link = Link(dve, dve_own)

                        def body(i):
                            if i is not None:
                                link.loop(i, dve_links)
                            for kind, u in seq:
                                if kind == "P":
                                    j = at[("Q", u, 0)]
                                    dve.wait_ge(pe_done.sem, val(i, J, base + j + 1))
                                    link(nc.vector.tensor_tensor(t_a[64:96], pair[j % 2][64:96], rot[64:96], ALU.mult))
                                    link(nc.vector.tensor_tensor(t_b[64:96], pair[j % 2][96:128], rot[96:128], ALU.mult))
                                    nc.vector.tensor_tensor(q_of(u)[64:96], t_a[64:96], t_b[64:96], ALU.add
                                                            ).then_inc(dve_free.sem, 1)
                                    dve.wait_ge(dve_free.sem, val(i, after["dve"][-1], b_e["dve"] + after["dve"][j]))
                                if kind == "A":
                                    for b in range(CH if causal else 2):
                                        j = at[("A", u, b)]
                                        dve.wait_ge(pe_done.sem, val(i, J, base + j + 1))
                                        if causal:
                                            ins = nc.vector.tensor_reduce(mx[:, u % 2, b:b + 1],
                                                                          pair[j % 2][:, 0:(b + 1) * P], AX.X, ALU.max)
                                        else:
                                            ins = nc.vector.tensor_reduce(
                                                mx[:, u % 2, 4 * b:4 * b + 4],
                                                pair[j % 2].rearrange("p (j k) -> p j k", k=MEM), AX.X, ALU.max)
                                        ins.then_inc(dve_free.sem, 1)
                                if kind == "R":
                                    j = at[("R", u, 0)]
                                    dve.wait_ge(pe_done.sem, val(i, J, base + j + 1))
                                    nc.vector.tensor_scalar(q_of(u)[dq:dq + 1], pair[j % 2][dq:dq + 1], -1.0, None,
                                                            ALU.mult).then_inc(dve_free.sem, 1)
                                if kind == "S":
                                    mine, other = slice(64 * (u % 2), 64 * (u % 2) + 64), slice(
                                        64 - 64 * (u % 2), 128 - 64 * (u % 2))
                                    for t in range(2):
                                        dve.wait_ge(pe_o.sem, val(i, len(steps), b_o + step_at[(u, t, last(t))] + 1))
                                        link(nc.vector.reciprocal(rec[mine], ps[other, 6 + t]))
                                        nc.vector.tensor_tensor(out_of(i, u)[:, HALF * t:HALF * (t + 1)],
                                                                ps[mine, 6 + t], rec[mine], ALU.mult
                                                                ).then_inc(dve_o.sem, 1)
                                        dve.wait_ge(dve_o.sem, val(i, 2 * U, b_do + 2 * u + t + 1))
                        looped(dve, body)
                        if iters > 1:
                            assert link.k == dve_links
                        dve_own.n += link.k * iters
            pe_done.n += J * iters
            act_free.n += after["act"][-1] * iters
            dve_free.n += after["dve"][-1] * iters
            pe_s.n += len(steps) * iters
            pe_o.n += len(steps) * iters
            act_p.n += len(steps) * iters
            dve_o.n += 2 * U * iters
            if causal:
                stream["slot"] += U * iters

        def memory_branch(layer, qm):
            with ExitStack() as scope:
                memT = sb_in(scope, "mem_in", [P, DT, MEM])
                km = sb_in(scope, "mem_k", [65, MEM_HEADS, MEM])
                vm = sb_in(scope, "mem_v", [P, MEM // P, MEM_HEADS, P])
                load(memT[:], a["mem"])
                with nc.Block() as block:
                    @block.vector
                    def _(dve):
                        nc.vector.memset(km[64:65], 1.0)
                        nc.vector.memset(vm[:], 1.0)
                linear(2, 8, lambda u, k, h: memT[:, k], ["act", "dve"],
                       heads_in_halves(lambda h: km[0:64, h]), ntok=MEM)

                def dest(c, op, src):
                    for par in range(2):
                        out = vm[:, c, par::2, 64 * par:64 * par + 64]
                        op(out, src.rearrange("p (a b d) -> p a b d", b=2, d=64)[:, :, par])
                token_major(MEM // P, MEM, DT, lambda k, c: memT[:, k, c * P:(c + 1) * P], dest)
                attention(1, MEM_HEADS, 64, MEM, 0.125, lambda u: qm[:, u], lambda u: km[:, u],
                          lambda u, s: vm[:, s, u],
                          lambda i, u: Z[64 * (u % 2):64 * (u % 2) + 64, 6 + u // 2], f"_m{layer}")

        def close_layer(layer, in_iters):
            with ExitStack() as scope:
                g = sb_in(scope, "gate2", [P, DT, T])
                linear(8, 8, from_h, ["act"] * 4, act_to(lambda m: g[:, m], ACT.Silu))
                with nc.Block() as block:
                    @block.vector
                    def _(dve):
                        for t in range(0, DT, 2):
                            nc.vector.tensor_tensor(Z[:, t], Z[:, t], g[:, t], ALU.mult)

                    @block.gpsimd
                    def _(pool):
                        for t in range(1, DT, 2):
                            nc.gpsimd.tensor_tensor(Z[:, t], Z[:, t], g[:, t], ALU.mult)

            def emit(e, link, m, u, src, i):
                return nc.vector.scalar_tensor_tensor(H[:, m], H[:, m], ALPHA, src, ALU.mult, ALU.add)
            linear(8, 8, from_merged, ["dve"] * (8 // in_iters), emit)
            with ExitStack() as scope:
                mean = sb_in(scope, "ln_mean", [P, T])
                base = pe_done.n
                with nc.Block() as block:
                    @block.tensor
                    def _(pe):
                        for t in range(DT):
                            for h in range(2):
                                mm = nc.tensor.matmul(pair[0][:, h * HALF:(h + 1) * HALF], ones,
                                                      H[:, t, h * HALF:(h + 1) * HALF], start=(t == 0),
                                                      stop=(t == DT - 1))
                        mm.then_inc(pe_done.sem, 1)

                    @block.vector
                    def _(dve):
                        dve.wait_ge(pe_done.sem, base + 1)
                        nc.vector.tensor_scalar(mean[:], pair[0], 1.0 / D, None, ALU.mult)
                pe_done.n += 1
                norm(lambda t: H[:, t], DT, 1, D, lambda t: V("ln_g", 8 * layer + t), lambda t: H[:, t],
                     bias=lambda t: V("ln_b", 8 * layer + t), center=mean[:])

        with ExitStack() as scope:
            rot = sb_in(scope, "rot", [P, T])
            cq = sb_in(scope, "cq", [P, 3, T])
            ckv = sb_in(scope, "ckv", [P, 2, T])
            qh = sb_in(scope, "qh", [QK + 1, 2, T])
            kh = sb_in(scope, "kh", [QK + 1, 2, T])
            vh = sb_in(scope, "vh", [P, 2, CH, P])
            up = slice(64, 128)
            with ExitStack() as s2:
                posi = sb_in(s2, "rope_pos", [P, T], I32)
                ang = sb_in(s2, "rope_ang", [P, T])
                turn = sb_in(s2, "rope_turn", [P, T])
                load(posi[up], a["pos"])
                b_dve = dve_out.n
                b_act = act_out.n
                with nc.Block() as block:
                    @block.vector
                    def _(dve):
                        link = Link(dve, dve_own)
                        link(nc.vector.tensor_copy(ang[up], posi[up]))
                        link(nc.vector.tensor_scalar(ang[up], ang[up], V("inv_freq")[up], None, ALU.mult))
                        link(nc.vector.tensor_scalar(turn[up], ang[up], 1.0 / TWO_PI, None, ALU.mult))
                        link(nc.vector.tensor_scalar(turn[up], turn[up], MAGIC, MAGIC, ALU.add, ALU.subtract))
                        link(nc.vector.scalar_tensor_tensor(ang[up], turn[up], -6.28125, ang[up], ALU.mult, ALU.add))
                        link(nc.vector.scalar_tensor_tensor(ang[up], turn[up], -(TWO_PI - 6.28125), ang[up], ALU.mult,
                                                            ALU.add))
                        nc.vector.tensor_scalar(ang[up], ang[up], 3.1415925, -3.1415925, ALU.min, ALU.max
                                                ).then_inc(dve_out.sem, 1)
                        dve.wait_ge(act_out.sem, b_act + 1)
                        link(nc.vector.tensor_tensor(rot[64:96], rot[64:96], rot[64:96], ALU.mult))
                        link(nc.vector.tensor_scalar(rot[64:96], rot[64:96], -2.0, 1.0, ALU.mult, ALU.add))
                        link(nc.vector.tensor_scalar(rot[96:128], rot[96:128], V("rope_sign")[96:128], None, ALU.mult))
                        nc.vector.memset(vh[:], 1.0)
                        nc.vector.memset(kh[QK:QK + 1], 1.0)
                        link.close()

                    @block.scalar
                    def _(act):
                        act.wait_ge(dve_out.sem, b_dve + 1)
                        nc.scalar.activation(rot[64:96], ang[64:96], ACT.Sin, scale=0.5)
                        nc.scalar.activation(rot[96:128], ang[96:128], ACT.Sin).then_inc(act_out.sem, 1)
                dve_out.n += 1
                act_out.n += 1
            with ExitStack() as s2:
                qm = sb_in(s2, "mla_qm", [65, MEM_HEADS, T])
                s3 = s2.enter_context(ExitStack())
                k_rope = sb_in(s3, "k_rope", [P, T])
                k_swap = sb_in(s3, "k_swap", [P, T])

                def emit(e, link, m, u, src, i):
                    if u < 5:
                        dest = cq[:, u] if u < 3 else ckv[:, u - 3]
                        if e == "act":
                            return nc.scalar.activation(dest, src, ACT.Copy)
                        return nc.vector.tensor_copy(dest, src)
                    if u == 5:
                        nc.vector.tensor_tensor(k_rope[64:96], src[64:96], rot[64:96], ALU.mult)
                        link(nc.vector.tensor_tensor(k_swap[64:96], src[96:128], rot[96:128], ALU.mult))
                        nc.vector.tensor_tensor(kh[64:96, 0], k_rope[64:96], k_swap[64:96], ALU.add)
                        return nc.vector.tensor_tensor(kh[64:96, 1], k_rope[64:96], k_swap[64:96], ALU.add)
                    return heads_in_halves(lambda h: qm[0:64, h])(e, link, u - 6, u, src, i)
                linear(8, 8, from_h, ["act", "dve", "act", "dve", "act", "dve", "act", "dve"], emit)
                s3.close()
                memory_branch(0, qm)
            norm(lambda t: cq[:, t], 3, 1, 384, lambda t: V("q_norm", t), lambda t: cq[:, t])
            norm(lambda t: ckv[:, t], 2, 1, 256, lambda t: V("kv_norm", t), lambda t: ckv[:, t])

            def project(pe, i, u, pair_of, s0):
                n = s0 + u
                value = 16 * (n // RING + 1)
                pe.wait_ge(w_full[n % RING].sem, value if i is None else i * 16 + value)
                slot = ring[:, n % RING]
                o = pair_of(("Q", u, 0))
                for k in range(3):
                    for h in range(2):
                        mm = nc.tensor.matmul(o[:, h * HALF:(h + 1) * HALF], slot[:, k], cq[:, k, h * HALF:(h + 1) * HALF],
                                              start=(k == 0), stop=(k == 2))
                mm.then_inc(pe_done.sem, 1)
                o = pair_of(("K", u, 0))
                for k in range(2):
                    for h in range(2):
                        mm = nc.tensor.matmul(o[0:64, h * HALF:(h + 1) * HALF], slot[:, 3 + k, 0:64],
                                              ckv[:, k, h * HALF:(h + 1) * HALF], start=(k == 0), stop=(k == 1))
                mm.then_inc(pe_done.sem, 1)
                o = pair_of(("V", u, 0))
                for c in range(CH):
                    for k in range(2):
                        mm = nc.tensor.matmul(o[:, c * 64:(c + 1) * 64], ckv[:, k, c * P:(c + 1) * P],
                                              slot[:, 3 + k, 64:128], start=(k == 0), stop=(k == 1))
                mm.then_inc(pe_done.sem, 1)

            def take(part, u, src):
                if part == "Q":
                    return nc.scalar.activation(qh[0:64, u % 2], src[0:64], ACT.Copy)
                if part == "K":
                    return nc.scalar.activation(kh[0:64, u % 2], src[0:64], ACT.Copy)
                return nc.scalar.activation(vh[:, u % 2, :, 64 * (u % 2):64 * (u % 2) + 64],
                                            src[:, 0:CH * 64].rearrange("p (c d) -> p c d", d=64), ACT.Copy)
            project.take = take
            attention(TOK_HEADS // 4, 4, QK, T, QK ** -0.5, lambda u: qh[:, u % 2], lambda u: kh[:, u % 2],
                      lambda u, s: vh[:, u % 2, s],
                      lambda i, u: Z[64 * (u % 2):64 * (u % 2) + 64, i * 2 + u // 2],
                      "_t", project=project)
        close_layer(0, 2)

        with ExitStack() as scope:
            xc = sb_in(scope, "lru_xc", [P, 6, T])
            with ExitStack() as s1:
                raw = sb_in(s1, "lru_raw", [P, 6, 3 + T])
                with ExitStack() as s2:
                    qm = sb_in(s2, "lru_qm", [65, MEM_HEADS, T])
                    zero_front(raw, 6)

                    def emit(e, link, m, u, src, i):
                        if u < 6:
                            if e == "act":
                                return nc.scalar.activation(raw[:, u, 3:3 + T], src, ACT.Copy)
                            return nc.vector.tensor_copy(raw[:, u, 3:3 + T], src)
                        return heads_in_halves(lambda h: qm[0:64, h])(e, link, u - 6, u, src, i)
                    linear(8, 8, from_h, ["act", "dve", "act", "dve", "act", "dve", "act", "dve"], emit)
                    memory_branch(1, qm)
                conv_silu(raw, 6, lambda tap, t: V("lru_conv_w", 6 * tap + t), lambda t: V("lru_conv_b", t), xc, None)
            r = sb_in(scope, "lru_r", [P, 6, T])
            ig = sb_in(scope, "lru_i", [P, 6, T])
            linear(12, 1, lambda u, k, h: xc[:, u % 6, h * HALF:(h + 1) * HALF], ["act"] * 12,
                   lambda e, link, m, u, src, i: nc.scalar.activation(
                       (r if u < 6 else ig)[:, u % 6], src, ACT.Sigmoid, bias=V("b_r" if u < 6 else "b_i", u % 6)))
            th = sb_in(scope, "lru_tanh", [P, 6, T])
            sp_ = sb_in(scope, "lru_sp", [P, 4, 6])
            b_act, b_dve, b_own = act_out.n, dve_out.n, act_own.n
            with nc.Block() as block:
                @block.vector
                def _(dve):
                    link = Link(dve, dve_own)
                    lam = V("lam", 0, 6)
                    nc.vector.scalar_tensor_tensor(sp_[:, 0], lam, -1.0, lam, ALU.mult, ALU.max).then_inc(dve_out.sem, 1)
                    link(nc.vector.tensor_scalar(sp_[:, 1], lam, -1.0, 0.0, ALU.mult, ALU.max))
                    dve.wait_ge(act_out.sem, b_act + 1)
                    link(nc.vector.tensor_tensor(sp_[:, 1], sp_[:, 1], sp_[:, 2], ALU.add))
                    link(nc.vector.tensor_scalar(sp_[:, 1], sp_[:, 1], -8.0, None, ALU.mult))
                    for t in range(6):
                        nc.vector.tensor_scalar(r[:, t], r[:, t], sp_[:, 1, t:t + 1], None, ALU.mult
                                                ).then_inc(dve_out.sem, 1)
                    for t in range(6):
                        dve.wait_ge(act_out.sem, b_act + 2 + t)
                        link(nc.vector.tensor_tensor(ig[:, t], ig[:, t], xc[:, t], ALU.mult))
                        link(nc.vector.tensor_tensor(xc[:, t], r[:, t], r[:, t], ALU.mult))
                        nc.vector.scalar_tensor_tensor(th[:, t], xc[:, t], 1.0, th[:, t], ALU.add, ALU.mult
                                                       ).then_inc(dve_out.sem, 1)
                    for t in range(6):
                        dve.wait_ge(act_out.sem, b_act + 8 + t)
                        link(nc.vector.tensor_tensor(ig[:, t], ig[:, t], th[:, t], ALU.mult))
                        nc.vector.tensor_tensor_scan(Z[:, t], r[:, t], ig[:, t], 0.0, ALU.mult, ALU.add)
                    link.close()

                @block.scalar
                def _(act):
                    act.wait_ge(dve_out.sem, b_dve + 1)
                    nc.scalar.activation(sp_[:, 3], sp_[:, 0], ACT.Exp, scale=-1.0).then_inc(act_own.sem, 1)
                    act.wait_ge(act_own.sem, b_own + 1)
                    nc.scalar.activation(sp_[:, 2], sp_[:, 3], ACT.Ln, bias=1.0).then_inc(act_out.sem, 1)
                    for t in range(6):
                        act.wait_ge(dve_out.sem, b_dve + 2 + t)
                        nc.scalar.activation(th[:, t], r[:, t], ACT.Tanh)
                        nc.scalar.activation(r[:, t], r[:, t], ACT.Exp).then_inc(act_out.sem, 1)
                    for t in range(6):
                        act.wait_ge(dve_out.sem, b_dve + 8 + t)
                        nc.scalar.activation(th[:, t], th[:, t], ACT.Sqrt, scale=-1.0).then_inc(act_out.sem, 1)
            act_own.n += 1
            act_out.n += 13
            dve_out.n += 13
        close_layer(1, 1)

        with nc.Block() as block:
            @block.sync
            def _(sp):
                sp.dma_start(a["out"], H[:]).then_inc(stored.sem, 16)
                stored.n += 16
                sp.wait_ge(stored.sem, stored.n)


def _tiles(w, ktp=None, at=0):
    k, m = w.shape
    kt = k // P
    out = np.zeros((ktp or kt, P, P), np.float32)
    out[:kt, :, at:at + m] = w.reshape(kt, P, m)
    return list(out)


def _cols(w, ktp=None):
    return [t for m in range(0, w.shape[1], P) for t in _tiles(w[:, m:m + P], ktp)]


def _wide(w):
    k, n = w.shape
    return list(w.reshape(k // P, P, n // P, P).transpose(0, 2, 1, 3).reshape(-1, P, P))


def _feature(v):
    return np.ascontiguousarray(v.reshape(-1, P).T)


def _pack(x):
    t, f = x.shape
    return np.ascontiguousarray(x.T.reshape(f // P, P, t).transpose(1, 0, 2))


def _block_pair(two):
    out = np.zeros((P, P), np.float32)
    out[:64, :64], out[64:, 64:] = two
    return out


def _stream(i):
    out = []

    def stage(tiles):
        out.extend(tiles)
        out.extend([np.zeros((P, P), np.float32)] * (-len(out) % SLOT))

    w = i["w_in"][0]
    at, parts = 0, []
    for n in (256, 256, 512, 16, 512, 256, 256, 512, 4, 4, 512, 512, 3072):
        parts.append(w[:, at:at + n])
        at += n
    gq, gk, gv, ga, gr, mq, mk, mv, mi, mf, mo, su, zg = parts
    stage(_cols(i["ada_w"][0]))
    misc = np.zeros((D, P), np.float32)
    misc[:, 0:16], misc[:, 32:36], misc[:, 64:68] = ga, mi, mf
    stage(_cols(gq) + _cols(gk) + _cols(misc))
    stage(_wide(gv))
    stage(_cols(gr))
    stage(_cols(zg[:, 0:D]))
    stage(_cols(i["proj_gla"][0]))
    stage(_cols(mq) + _cols(mk))
    stage(_wide(mv))
    stage(_cols(mo))
    stage(_cols(zg[:, D:2 * D]))
    stage(_cols(i["proj_ml"][0]))
    stage(_cols(su))
    stage(_cols(i["s5_glu_w"][0]))
    stage(_cols(zg[:, 2 * D:]))
    stage(_cols(i["proj_s5"][0]))
    stage(_cols(i["w_out"][0]))
    f = i["ffn_w_in"][0]
    stage([t for m in range(0, FFN, P) for o in (0, FFN) for t in _tiles(f[:, o + m:o + m + P])])
    stage(_cols(i["ffn_w_out"][0], 24))

    w = i["mla_w_in_2"][0]
    wq, wkv, wr, wg, wm = (w[:, lo:hi] for lo, hi in ((0, 384), (384, 640), (640, 672), (672, 1696), (1696, 1952)))
    swap = np.r_[16:32, 0:16]
    stage(_cols(wq) + _cols(wkv) + _tiles(np.concatenate([wr, wr[:, swap]], 1), at=64) + _cols(wm))
    stage(_cols(i["w_mem_kv_2"][0][:, :256]))
    stage(_wide(i["w_mem_kv_2"][0][:, 256:]))
    uq = i["mla_w_uq_2"][0].reshape(384, TOK_HEADS, QK)
    ukv = i["mla_w_ukv_2"][0].reshape(256, TOK_HEADS, 128)
    for h in range(TOK_HEADS):
        stage(_tiles(np.concatenate([uq[:, h], uq[:, h, 64:][:, swap]], 1)) + _tiles(ukv[:, h]))
    stage(_cols(wg))
    stage(_cols(i["w_out_2"][0]))

    w = i["lru_w_in_2"][0]
    stage(_cols(w[:, :768]) + _cols(w[:, 1792:]))
    stage(_cols(i["w_mem_kv_2"][1][:, :256]))
    stage(_wide(i["w_mem_kv_2"][1][:, 256:]))
    stage([_block_pair(i[n][0][2 * t:2 * t + 2]) for n in ("lru_w_rgate_2", "lru_w_igate_2") for t in range(6)])
    stage(_cols(w[:, 768:1792]))
    stage(_cols(i["w_out_2"][1]))
    return out


def _vectors(i):
    out = np.zeros((P, NVEC), np.float32)

    def put(name, v):
        at, n = VEC[name]
        out[:, at:at + n] = _feature(v)

    for name, key in [("c", "c"), ("ada_b", "ada_b"), ("pre1_w", "pre1_w"), ("post1_w", "post1_w"),
                      ("pre2_w", "pre2_w"), ("post2_w", "post2_w"), ("gla_a_b", "gla_a_b"),
                      ("gla_norm_w", "gla_norm_w"), ("conv_w", "ml_conv_w"), ("conv_b", "ml_conv_b"),
                      ("s5_d", "s5_d"), ("glu_b", "s5_glu_b"), ("gate_b", "branch_gate_b"),
                      ("lam_re", "s5_lam_re"), ("lam_im", "s5_lam_im"), ("q_norm", "mla_q_norm_2"),
                      ("kv_norm", "mla_kv_norm_2"), ("lru_conv_w", "lru_conv_w_2"),
                      ("lru_conv_b", "lru_conv_b_2"), ("b_r", "lru_b_rgate_2"), ("b_i", "lru_b_igate_2"),
                      ("lam", "lru_lambda_2"), ("ln_g", "ln_g_2"), ("ln_b", "ln_b_2")]:
        put(name, i[key])
    put("log_step", np.repeat(i["s5_log_step"][0], 64))
    out[0:HEADS, VEC["i_b"][0]] = i["ml_i_b"][0]
    out[0:HEADS, VEC["f_b"][0]] = i["ml_f_b"][0]
    half = np.float32(10000.0) ** (-np.arange(16, dtype=np.float32) / np.float32(16))
    out[64:128, VEC["inv_freq"][0]] = np.tile(half, 4)
    out[96:128, VEC["rope_sign"][0]] = np.repeat(np.float32([-1, 1]), 16)
    return out


def _constant_array():
    out = np.zeros((P, NCONST), np.float32)
    j, i = np.arange(P)[:, None], np.arange(P)[None]

    def put(name, v):
        at, n = CONST[name]
        out[:, at:at + n] = v
    put("ident", j == i)
    put("diag", j == i)
    put("ones", 1.0)
    put("mask_qk", np.where(i <= j, 0.0, -BIG))
    put("mask_kq", np.where(j <= i, 0.0, -BIG))
    put("sel", np.arange(P)[:, None] == np.arange(HEADS * P)[None] // P)
    put("ramp", np.arange(32)[None])
    return out


def _gla_masks():
    j, i = np.arange(P)[:, None, None], np.arange(P)[None, None]
    half = (1 << np.arange(7))[None, :, None]
    same = j // (2 * half) == i // (2 * half)
    return (same & (j % (2 * half) < half) & (i % (2 * half) >= half)).astype(np.int32)


def _s5_blocks(re, im):
    out = np.zeros((2, 64, 2, 16, 2, 16), np.float32)
    for r, m in enumerate((re, im)):
        m = m.reshape(16, 2, 64, 16)
        for g in range(2):
            out[g, :, r, :, g] = m[:, g].transpose(1, 0, 2)
    return out.reshape(P, 2, 16, 32)


def _layout(i):
    i = {k: np.asarray(v) for k, v in i.items()}
    tiles = np.stack(_stream(i))
    w = np.ascontiguousarray(tiles.reshape(-1, SLOT, P, P).transpose(0, 2, 1, 3)).reshape(-1, P, SLOT * P)
    return {
        "w": w,
        "vec": _vectors(i),
        "cst": _constant_array(),
        "x": _pack(i["x"][0]),
        "masks": _gla_masks(),
        "mem": _pack(i["mem_2"][0]),
        "pos": np.ascontiguousarray(np.broadcast_to(i["positions_2"], (64, T))),
        "gla_a2": np.ascontiguousarray(i["gla_a2"][0]),
        "s5_b": _s5_blocks(i["s5_b_re"][0], i["s5_b_im"][0]),
        "s5_c": _s5_blocks(i["s5_c_re"][0].transpose(0, 2, 1), i["s5_c_im"][0].transpose(0, 2, 1)),
    }


def kernel(**inputs):
    import concourse.bacc as bacc
    from concourse.bass_utils import run_bass_kernel_spmd

    arrays = _layout(inputs)
    nc = bacc.Bacc("TRN2", target_bir_lowering=False, num_devices=1)
    a = {name: nc.dram_tensor(f"in_{name}", v.shape, mybir.dt.from_np(v.dtype), kind="ExternalInput").ap()
         for name, v in arrays.items()}
    a["out"] = nc.dram_tensor("out_y", (P, DT, T), F32, kind="ExternalOutput").ap()
    build(nc, a)
    r = run_bass_kernel_spmd(nc, [{f"in_{name}": v for name, v in arrays.items()}], core_ids=[0])
    y = r.results[0]["out_y"].reshape(P, DT, T)
    return np.ascontiguousarray(y.transpose(2, 1, 0)).reshape(1, T, D)
```
